# Optimizing a Trainium2 kernel written in Bass

```python
import jax
import jax.numpy as jnp
from jax import lax
import numpy as np

D_MODEL = 1024
BATCH = 1
SEQ = 1024
DEPTH = 1
DEC_BATCH = 8
DEC_SEQ = 16
PAST_LEN = 256

CHUNK = 64
EPS = 1e-6
NEG_INF = -1e30

N_HEADS_A = 8
N_KV_A = 2
GROUP_A = N_HEADS_A // N_KV_A
HEAD_DIM_A = 64
WINDOW = 128
WIN_CHUNKS = WINDOW // CHUNK
BAND = (WIN_CHUNKS + 1) * CHUNK

N_HEADS_B = 4
DK_B = 128
DV_B = 256

Q_A = N_HEADS_A * HEAD_DIM_A
KV_A = N_KV_A * HEAD_DIM_A
Q_B = N_HEADS_B * DK_B
V_B = N_HEADS_B * DV_B
D_IN = Q_A + 2 * KV_A + 2 * Q_B + 2 * V_B + 2 * D_MODEL
SPLITS = (Q_A,
          Q_A + KV_A,
          Q_A + 2 * KV_A,
          Q_A + 2 * KV_A + Q_B,
          Q_A + 2 * KV_A + 2 * Q_B,
          Q_A + 2 * KV_A + 2 * Q_B + V_B,
          Q_A + 2 * KV_A + 2 * Q_B + 2 * V_B)

N_KEYS = 128
N_EXPERTS = N_KEYS * N_KEYS
PEER_HEADS = 8
PEER_QDIM = 256
PEER_HALF = PEER_QDIM // 2
PEER_TOPK = 16
PEER_BLOCK = 128

kernel_name = 'streaming_swa_retention_peer_step'

def rmsnorm(x, g):
    xf = x.astype(jnp.float32)
    y = xf * lax.rsqrt(jnp.mean(xf * xf, axis=-1, keepdims=True) + EPS)
    return y.astype(x.dtype) * g

def alibi_slopes():
    return 2.0 ** (-8.0 * jnp.arange(1, N_HEADS_A + 1, dtype=jnp.float32) / N_HEADS_A)

def retention_log_decay():
    return jnp.log1p(-(2.0 ** (-5.0 - jnp.arange(N_HEADS_B, dtype=jnp.float32))))

def project(h, w_in, b_gate):
    lead = h.shape[:-1]
    z = h @ w_in
    qa, ka, va, qb, kb, vb, rg, bg = jnp.split(z, SPLITS, axis=-1)
    ga, gb = jnp.split(bg + b_gate, 2, axis=-1)
    qa = qa.reshape(*lead, N_KV_A, GROUP_A, HEAD_DIM_A)
    ka = ka.reshape(*lead, N_KV_A, HEAD_DIM_A)
    va = va.reshape(*lead, N_KV_A, HEAD_DIM_A)
    qb = qb.reshape(*lead, N_HEADS_B, DK_B)
    kb = kb.reshape(*lead, N_HEADS_B, DK_B) * (DK_B ** -0.5)
    vb = vb.reshape(*lead, N_HEADS_B, DV_B)
    rg = rg.reshape(*lead, N_HEADS_B, DV_B)
    return qa, ka, va, qb, kb, vb, rg, ga, gb

def swa_attend(q, k, v, q_pos, k_pos, k_valid, sinks):
    s = jnp.einsum('...qkgd,...skd->...kgqs', q, k).astype(jnp.float32) * (HEAD_DIM_A ** -0.5)
    qp = q_pos[..., :, None]
    kp = k_pos[..., None, :]
    dist = jnp.abs(qp - kp).astype(jnp.float32)
    slopes = alibi_slopes().reshape(N_KV_A, GROUP_A, 1, 1)
    s = s - slopes * dist[..., None, None, :, :]
    qc = qp // CHUNK
    kc = kp // CHUNK
    allowed = k_valid[..., None, :] & (kc <= qc) & (kc >= qc - WIN_CHUNKS)
    s = jnp.where(allowed[..., None, None, :, :], s, NEG_INF)
    sink = sinks.astype(jnp.float32).reshape(N_KV_A, GROUP_A, 1, 1)
    m = jnp.maximum(jnp.max(s, axis=-1, keepdims=True), sink)
    p = jnp.exp(s - m)
    denom = jnp.sum(p, axis=-1, keepdims=True) + jnp.exp(sink - m)
    p = (p / denom).astype(v.dtype)
    return jnp.einsum('...kgqs,...skd->...qkgd', p, v)

def swa_prompt(qa, ka, va, sinks):
    b, s_len = ka.shape[:2]
    n_c = s_len // CHUNK
    q = qa.reshape(b, n_c, CHUNK, N_KV_A, GROUP_A, HEAD_DIM_A)
    pad = ((0, 0), (WIN_CHUNKS * CHUNK, 0), (0, 0), (0, 0))
    kp = jnp.pad(ka, pad).reshape(b, n_c + WIN_CHUNKS, CHUNK, N_KV_A, HEAD_DIM_A)
    vp = jnp.pad(va, pad).reshape(b, n_c + WIN_CHUNKS, CHUNK, N_KV_A, HEAD_DIM_A)
    k_band = jnp.concatenate([kp[:, j:j + n_c] for j in range(WIN_CHUNKS + 1)], axis=2)
    v_band = jnp.concatenate([vp[:, j:j + n_c] for j in range(WIN_CHUNKS + 1)], axis=2)
    q_pos = jnp.arange(s_len, dtype=jnp.int32).reshape(n_c, CHUNK)
    k_pos = (jnp.arange(n_c, dtype=jnp.int32)[:, None] - WIN_CHUNKS) * CHUNK + jnp.arange(BAND, dtype=jnp.int32)[None, :]
    o = swa_attend(q, k_band, v_band, q_pos, k_pos, k_pos >= 0, sinks)
    return o.reshape(b, s_len, Q_A), ka[:, s_len - WINDOW:], va[:, s_len - WINDOW:]

def swa_sample(qa, ka, va, cache_k, cache_v, sinks):
    b, n_new = ka.shape[:2]
    k_all = jnp.concatenate([cache_k.astype(ka.dtype), ka], axis=1)
    v_all = jnp.concatenate([cache_v.astype(va.dtype), va], axis=1)
    q_pos = PAST_LEN + jnp.arange(n_new, dtype=jnp.int32)
    k_pos = jnp.concatenate([PAST_LEN - WINDOW + jnp.arange(WINDOW, dtype=jnp.int32), q_pos])
    o = swa_attend(qa, k_all, v_all, q_pos, k_pos, k_pos >= 0, sinks)
    return o.reshape(b, n_new, Q_A), k_all[:, n_new:], v_all[:, n_new:]

def retention_chunk(q, k, v, state):
    n_len = q.shape[1]
    lg = retention_log_decay()
    n = jnp.arange(n_len, dtype=jnp.float32)
    diff = n[:, None] - n[None, :]
    intra = jnp.where(diff >= 0, jnp.exp(jnp.maximum(diff, 0.0) * lg[:, None, None]), 0.0)
    qf = q.astype(jnp.float32)
    kf = k.astype(jnp.float32)
    vf = v.astype(jnp.float32)
    st = state.astype(jnp.float32)
    scores = jnp.einsum('blhd,bmhd->bhlm', qf, kf) * intra
    o = jnp.einsum('bhlm,bmhv->blhv', scores, vf)
    o = o + jnp.einsum('blhd,bhdv->blhv', qf, st) * jnp.exp((n[:, None] + 1.0) * lg)[None, :, :, None]
    k_dec = kf * jnp.exp((n_len - 1.0 - n)[:, None] * lg)[None, :, :, None]
    new_state = jnp.exp(n_len * lg)[None, :, None, None] * st + jnp.einsum('blhd,blhv->bhdv', k_dec, vf)
    return o, new_state

def retention_prompt(qb, kb, vb):
    b, s_len = qb.shape[:2]
    n_c = s_len // CHUNK

    def to_chunks(a):
        return jnp.swapaxes(a.reshape(b, n_c, CHUNK, *a.shape[2:]), 0, 1)

    def step(carry, inp):
        qi, ki, vi = inp
        o, carry = retention_chunk(qi, ki, vi, carry)
        return carry, o

    s0 = jnp.zeros((b, N_HEADS_B, DK_B, DV_B), jnp.float32)
    s_fin, o = lax.scan(step, s0, (to_chunks(qb), to_chunks(kb), to_chunks(vb)))
    return jnp.swapaxes(o, 0, 1).reshape(b, s_len, N_HEADS_B, DV_B), s_fin

def retention_output(o, rg):
    mu = jnp.mean(o, axis=-1, keepdims=True)
    var = jnp.mean(jnp.square(o - mu), axis=-1, keepdims=True)
    on = ((o - mu) * lax.rsqrt(var + EPS)).astype(rg.dtype)
    y = on * jax.nn.silu(rg)
    return y.reshape(*y.shape[:-2], V_B)

def merge_branches(oa, ob, ga, gb, w_branch_a, w_branch_b, w_out):
    mix = jax.nn.sigmoid(ga) * (oa @ w_branch_a) + jax.nn.sigmoid(gb) * (ob @ w_branch_b)
    return mix @ w_out

def peer_ffn(h, w_q, sub_k1, sub_k2, expert_u, expert_v):
    lead = h.shape[:-1]
    ht = h.reshape(-1, D_MODEL)
    n_tok = ht.shape[0]
    n_blk = -(-n_tok // PEER_BLOCK)
    ht = jnp.pad(ht, ((0, n_blk * PEER_BLOCK - n_tok), (0, 0)))
    q = (ht @ w_q).reshape(-1, PEER_HEADS, PEER_QDIM)
    s1 = jnp.einsum('thd,nd->thn', q[..., :PEER_HALF], sub_k1).astype(jnp.float32)
    s2 = jnp.einsum('thd,nd->thn', q[..., PEER_HALF:], sub_k2).astype(jnp.float32)
    v1, i1 = lax.top_k(s1, PEER_TOPK)
    v2, i2 = lax.top_k(s2, PEER_TOPK)
    cand = (v1[..., :, None] + v2[..., None, :]).reshape(-1, PEER_HEADS, PEER_TOPK * PEER_TOPK)
    cidx = (i1[..., :, None] * N_KEYS + i2[..., None, :]).reshape(-1, PEER_HEADS, PEER_TOPK * PEER_TOPK)
    best, pos = lax.top_k(cand, PEER_TOPK)
    idx = jnp.take_along_axis(cidx, pos, axis=-1)
    gate = jax.nn.softmax(best, axis=-1).astype(h.dtype)

    def expert_block(args):
        hb, ib, gb = args
        u = jnp.take(expert_u, ib, axis=0)
        act = jax.nn.gelu(jnp.einsum('td,tkd->tk', hb, u))
        vrows = jnp.take(expert_v, ib, axis=0)
        return jnp.einsum('tk,tkd->td', gb * act, vrows)

    y = lax.map(expert_block, (ht.reshape(n_blk, PEER_BLOCK, D_MODEL),
                               idx.reshape(n_blk, PEER_BLOCK, PEER_HEADS * PEER_TOPK),
                               gate.reshape(n_blk, PEER_BLOCK, PEER_HEADS * PEER_TOPK)))
    return y.reshape(-1, D_MODEL)[:n_tok].reshape(*lead, D_MODEL)

def setup_inputs(seed: int = 0) -> dict:
    key = jax.random.key(seed)
    ks = jax.random.split(key, 20)
    f32 = jnp.float32

    def nrm(k, shape, scale):
        return jax.random.normal(k, shape, f32) * scale

    return {
        'x_prompt': nrm(ks[0], (BATCH, SEQ, D_MODEL), 1.0),
        'x_sample': nrm(ks[1], (DEC_BATCH, DEC_SEQ, D_MODEL), 1.0),
        'cache_swa_k': nrm(ks[2], (DEPTH, DEC_BATCH, WINDOW, N_KV_A, HEAD_DIM_A), 1.0),
        'cache_swa_v': nrm(ks[3], (DEPTH, DEC_BATCH, WINDOW, N_KV_A, HEAD_DIM_A), 1.0),
        'state_ret': nrm(ks[4], (DEPTH, DEC_BATCH, N_HEADS_B, DK_B, DV_B), 0.5),
        'norm_mix': 1.0 + nrm(ks[5], (DEPTH, D_MODEL), 0.01),
        'w_in': nrm(ks[6], (DEPTH, D_MODEL, D_IN), D_MODEL ** -0.5),
        'b_gate': nrm(ks[7], (DEPTH, 2 * D_MODEL), 0.02),
        'attn_sinks': nrm(ks[8], (DEPTH, N_HEADS_A), 0.5),
        'w_branch_a': nrm(ks[9], (DEPTH, Q_A, D_MODEL), Q_A ** -0.5),
        'w_branch_b': nrm(ks[10], (DEPTH, V_B, D_MODEL), V_B ** -0.5),
        'w_out': nrm(ks[11], (DEPTH, D_MODEL, D_MODEL), D_MODEL ** -0.5),
        'norm_ffn': 1.0 + nrm(ks[12], (DEPTH, D_MODEL), 0.01),
        'peer_w_q': nrm(ks[13], (DEPTH, D_MODEL, PEER_HEADS * PEER_QDIM), D_MODEL ** -0.5),
        'peer_sub_k1': nrm(ks[14], (DEPTH, N_KEYS, PEER_HALF), PEER_HALF ** -0.5),
        'peer_sub_k2': nrm(ks[15], (DEPTH, N_KEYS, PEER_HALF), PEER_HALF ** -0.5),
        'peer_u': nrm(ks[16], (DEPTH, N_EXPERTS, D_MODEL), D_MODEL ** -0.5),
        'peer_v': nrm(ks[17], (DEPTH, N_EXPERTS, D_MODEL), PEER_HEADS ** -0.5),
        'norm_final': 1.0 + nrm(ks[18], (D_MODEL,), 0.01),
    }

def reference(x_prompt, x_sample, cache_swa_k, cache_swa_v, state_ret,
              norm_mix, w_in, b_gate, attn_sinks, w_branch_a, w_branch_b, w_out,
              norm_ffn, peer_w_q, peer_sub_k1, peer_sub_k2, peer_u, peer_v, norm_final):
    xp = x_prompt
    xs = x_sample
    kp_rows, vp_rows, sp_fin, ks_rows, vs_rows, ss_fin = [], [], [], [], [], []
    for l in range(DEPTH):
        h = rmsnorm(xp, norm_mix[l])
        qa, ka, va, qb, kb, vb, rg, ga, gb = project(h, w_in[l], b_gate[l])
        oa, k_new, v_new = swa_prompt(qa, ka, va, attn_sinks[l])
        ob, s_new = retention_prompt(qb, kb, vb)
        ob = retention_output(ob, rg)
        xp = xp + merge_branches(oa, ob, ga, gb, w_branch_a[l], w_branch_b[l], w_out[l])
        xp = xp + peer_ffn(rmsnorm(xp, norm_ffn[l]), peer_w_q[l], peer_sub_k1[l], peer_sub_k2[l], peer_u[l], peer_v[l])
        kp_rows.append(k_new)
        vp_rows.append(v_new)
        sp_fin.append(s_new)
        h = rmsnorm(xs, norm_mix[l])
        qa, ka, va, qb, kb, vb, rg, ga, gb = project(h, w_in[l], b_gate[l])
        oa, k_new, v_new = swa_sample(qa, ka, va, cache_swa_k[l], cache_swa_v[l], attn_sinks[l])
        ob, s_new = retention_chunk(qb, kb, vb, state_ret[l])
        ob = retention_output(ob, rg)
        xs = xs + merge_branches(oa, ob, ga, gb, w_branch_a[l], w_branch_b[l], w_out[l])
        xs = xs + peer_ffn(rmsnorm(xs, norm_ffn[l]), peer_w_q[l], peer_sub_k1[l], peer_sub_k2[l], peer_u[l], peer_v[l])
        ks_rows.append(k_new)
        vs_rows.append(v_new)
        ss_fin.append(s_new)
    y_prompt = rmsnorm(xp, norm_final)
    y_sample = rmsnorm(xs, norm_final)
    return (y_prompt, y_sample,
            jnp.stack(kp_rows), jnp.stack(vp_rows), jnp.stack(sp_fin),
            jnp.stack(ks_rows), jnp.stack(vs_rows), jnp.stack(ss_fin))


_drawn_inputs = setup_inputs


def setup_inputs(seed=0):
    import zlib

    import numpy as np

    out = dict(_drawn_inputs(seed))
    spreads = {}
    factors = {'norm_mix': 3.317,
     'b_gate': 5.9,
     'attn_sinks': 33.064,
     'norm_ffn': 12.088,
     'norm_final': 33.398}
    for name, (base, spread) in spreads.items():
        noise = np.random.default_rng([zlib.crc32(name.encode()), seed]).standard_normal(out[name].shape)
        drawn = base * np.exp(spread * noise) if base else spread * noise
        out[name] = jnp.asarray(drawn.astype(out[name].dtype))
    for name, factor in factors.items():
        out[name] = (out[name] * factor).astype(out[name].dtype)
    return out
```

```python
import math
from contextlib import ExitStack

import concourse.bass as bass
import numpy as np
from concourse import mybir

P = 128
D = 1024
KT = D // P
SEQ, DEC_B, DEC_S = 1024, 8, 16
NB = 1 + SEQ // P
CHUNK, WINDOW, EPS, NEG = 64, 128, 1e-6, -1e30
HA, KV, GRP, HD = 8, 2, 4, 64
HB, DK, DV = 4, 128, 256
QA, KA, VA, QB, KB, VB, RG, GA, GB, D_IN = (0, 512, 640, 768, 1280, 1792, 2816, 3840, 4864, 5888)
WT = 16
WC = D_IN // WT
NKEY, PH, TOPK = 128, 8, 16
NEXP = NKEY * NKEY
NK = PH * TOPK
RING = 16
LOW = -3.0e38
LOG_DECAY = [math.log1p(-(2.0 ** (-5.0 - h))) for h in range(HB)]

f32 = mybir.dt.float32
u32 = mybir.dt.uint32
ALU = mybir.AluOpType
ACT = mybir.ActivationFunctionType
AX = mybir.AxisListType


def shape_tables():
    q = np.arange(P)[:, None].astype(np.float64)
    slopes = 2.0 ** -(np.arange(HA) + 1.0)
    k = np.arange(2 * P)[None, :]
    dist = np.abs(P + q - k)
    seen = ((q < CHUNK) & (k < 3 * CHUNK)) | ((q >= CHUNK) & (k >= CHUNK))
    alibi = np.where(seen[:, None, :], -slopes[None, :, None] * dist[:, None, :], NEG)
    row = np.arange(P)
    ks = np.arange(WINDOW + DEC_S)[None, :]
    alibi_s = -slopes[row // DEC_S][:, None] * np.abs(WINDOW + (row % DEC_S)[:, None] - ks)
    lg = np.array(LOG_DECAY)
    m, n = np.arange(P)[:, None], np.arange(P)[None, :]
    intra = np.stack([np.where(n >= m, np.exp((n - m) * g), 0.0) for g in lg], 1) * DK ** -0.5
    same = (m // DEC_S) == (n // DEC_S)
    intra_s = intra * same[:, None, :]
    into = np.exp((np.arange(P) + 1.0)[None, :] * lg[:, None])
    into_s = np.exp((np.arange(P) % DEC_S + 1.0)[None, :] * lg[:, None])
    out = np.exp((P - 1.0 - np.arange(P))[:, None] * lg[None, :]) * DK ** -0.5
    out_s = np.exp((DEC_S - 1.0 - np.arange(P) % DEC_S)[:, None] * lg[None, :]) * DK ** -0.5
    out_s = out_s[:, None, :] * (np.arange(P)[:, None, None] // DEC_S == np.arange(DEC_B)[None, :, None])
    t = {
        "ident": np.eye(P), "alibi": alibi, "alibi_s": alibi_s, "intra": intra, "intra_s": intra_s,
        "into": np.broadcast_to(into[None], (P, HB, P)), "into_s": np.broadcast_to(into_s[None], (P, HB, P)),
        "out_dec": out, "out_dec_s": out_s, "iota16": np.broadcast_to(np.arange(TOPK)[None, :], (P, TOPK)),
    }
    return {n: np.ascontiguousarray(a.reshape(P, -1).astype(np.float32)) for n, a in t.items()}


class Steps:

    def __init__(self, eng, sem, base=0):
        self.eng, self.sem, self.base, self.n = eng, sem, base, 0

    def did(self, ins):
        ins.then_inc(self.sem, 1)
        self.n += 1

    def settle(self):
        self.eng.wait_ge(self.sem, self.base + self.n)


DVE_B = 2
DVE_C = 15
STEPS_C = 1 + (NB - 1) * DVE_B


def trunk_kernel(nc, t, o):
    V, S, G, T = nc.vector, nc.scalar, nc.gpsimd, nc.tensor
    ctx = ExitStack()
    with ctx:
        def sb(stack, name, shape, dt=f32):
            return stack.enter_context(nc.sbuf_tensor(name, shape, dt))

        def sem(name):
            return ctx.enter_context(nc.semaphore(name))

        def dram(name, shape, dt=f32):
            return nc.dram_tensor(name, shape, dt, kind="Internal").ap()

        z_d = dram("z_d", (NB * P, D_IN))
        x1_d = dram("x1_d", (NB * P, D))
        h2_d = dram("h2_d", (NB * P, D))
        idx_d = dram("idx_d", (NB * P, NK), u32)
        gate_d = dram("gate_d", (NB * P, NK))

        ps = ctx.enter_context(nc.psum_tensor("ps", [P, 8, 512], f32))
        ident = sb(ctx, "ident", [P, P])
        s_const = sem("s_const")

        def bank(b, n=1):
            return ps[:, b:b + n, :].rearrange("p b n -> p (b n)")

        def rows(ap, blk):
            return ap[bass.ds(blk * P, P), :] if not isinstance(blk, int) else ap[blk * P:(blk + 1) * P, :]

        s_xt, s_x, s_g = sem("s_xt"), sem("s_x"), sem("s_g")
        s_w = [sem(f"s_w{i}") for i in range(2)]
        s_ssq, s_ms, s_sq, s_rstd, s_xg = sem("s_ssq"), sem("s_ms"), sem("s_sq"), sem("s_rstd"), sem("s_xg")
        s_mm = sem("s_mm")
        s_zact, s_zdve = sem("s_zact"), sem("s_zdve")
        s_zst = [sem(f"s_zst{i}") for i in range(2)]
        s_zfree = [sem(f"s_zfree{i}") for i in range(2)]
        s_pool, s_sp = sem("s_pool"), sem("s_sp")
        AB = 6

        with ExitStack() as a:
            xg = sb(a, "xg", [P, KT, NB * P])
            xn = sb(a, "xn", [P, NB, D])
            gm = sb(a, "gm", [P, KT])
            w = sb(a, "w", [P, 2, KT, WC])
            zo = sb(a, "zo", [P, 2, NB, WC])
            ssq = sb(a, "ssq", [P, NB])
            rstd = sb(a, "rstd", [P, NB])
            junk = sb(a, "junk", [P, 2, D])
            z_t = z_d.rearrange("(b p) c -> p b c", p=P)
            w_t = t["w_in"].rearrange("(t p) n -> t p n", p=P)
            with nc.Block() as block:
                @block.sync
                def _(sp):
                    sp.dma_start(gm[:], t["norm_mix"]).then_inc(s_g, 16)
                    for k in range(KT):
                        sp.dma_start(xg[:, k, :], t["x_t"][k * P:(k + 1) * P, :]).then_inc(s_xt, 16)
                    sp.dma_start(xn[:], t["x"].rearrange("(b p) d -> p b d", p=P)).then_inc(s_x, 16)
                    sp.dma_start(ident[:], t["ident"]).then_inc(s_const, 16)
                    sp.sem_inc(s_zfree[0], 1)
                    sp.sem_inc(s_zfree[1], 1)
                    with sp.Fori(0, WT // 2) as i:
                        for p in range(2):
                            sp.wait_ge(s_zact, NB * i + (5 if p == 0 else 9) + AB // 2)
                            sp.sem_inc(s_sp, 1)
                            sp.wait_ge(s_zdve, NB * i + (4 if p == 0 else 9) + AB // 2)
                            sp.sem_inc(s_sp, 1)
                            sp.dma_start(z_t[:, :, bass.ds((2 * i + p) * WC, WC)], zo[:, p]).then_inc(s_zst[p], 16)
                            sp.wait_ge(s_zst[p], 16 * i + 16)
                            sp.sem_inc(s_zfree[p], 1)

                @block.gpsimd
                def _(g):
                    for p in range(2):
                        g.dma_start(w[:, p].rearrange("p k c -> p (k c)"), t["w_in"][p * P:(p + 1) * P, :]).then_inc(s_w[p], 16)
                    with g.Fori(1, WT // 2) as i:
                        for p in range(2):
                            g.wait_ge(s_mm, NB * (2 * i + p - 1))
                            g.sem_inc(s_pool, 1)
                            g.dma_start(w[:, p].rearrange("p k c -> p (k c)"),
                                        t["w_in"][bass.ds((2 * i + p) * P, P), :]).then_inc(s_w[p], 16)

                @block.scalar
                def _(act):
                    act.wait_ge(s_x, 16)
                    for b in range(NB):
                        if b >= 2:
                            act.wait_ge(s_ssq, b - 1)
                        S.activation(junk[:, b % 2, :], xn[:, b, :], ACT.Square, accum_out=ssq[:, b:b + 1]).then_inc(s_ssq, 1)
                    act.wait_ge(s_ms, 1)
                    S.activation(rstd[:], ssq[:], ACT.Sqrt).then_inc(s_sq, 1)
                    act.wait_ge(s_rstd, 1)
                    act.sem_inc(s_zact, AB // 2)
                    with act.Fori(0, WT // 2) as i:
                        for n in range(0, 2 * NB, 2):
                            if n in (0, 10):
                                act.wait_ge(s_zfree[n // NB], i + 1)
                            act.wait_ge(s_mm, 2 * NB * i + n + 1)
                            S.activation(zo[:, n // NB, n % NB, :], ps[:, n % AB, 0:WC], ACT.Copy,
                                         scale=rstd[:, n % NB:n % NB + 1]).then_inc(s_zact, 1)

                @block.vector
                def _(v):
                    v.wait_ge(s_g, 16)
                    for k in range(KT):
                        v.wait_ge(s_xt, 16 * KT)
                        V.tensor_scalar(xg[:, k, :], xg[:, k, :], gm[:, k:k + 1], None, ALU.mult).then_inc(s_xg, 1)
                    v.wait_ge(s_ssq, NB)
                    V.tensor_scalar(ssq[:], ssq[:], 1.0 / D, EPS, ALU.mult, ALU.add).then_inc(s_ms, 1)
                    v.wait_ge(s_sq, 1)
                    V.reciprocal(rstd[:], rstd[:]).then_inc(s_rstd, 1)
                    v.wait_ge(s_rstd, 1)
                    v.sem_inc(s_zdve, AB // 2)
                    with v.Fori(0, WT // 2) as i:
                        for n in range(1, 2 * NB, 2):
                            if n in (1, 9):
                                v.wait_ge(s_zfree[n // NB], i + 1)
                            v.wait_ge(s_mm, 2 * NB * i + n + 1)
                            V.tensor_scalar(zo[:, n // NB, n % NB, :], ps[:, n % AB, 0:WC],
                                            rstd[:, n % NB:n % NB + 1], None, ALU.mult).then_inc(s_zdve, 1)

                @block.tensor
                def _(pe):
                    pe.wait_ge(s_xg, KT)
                    with pe.Fori(0, WT // 2) as i:
                        for n in range(2 * NB):
                            p, b = n // NB, n % NB
                            if b == 0:
                                pe.wait_ge(s_w[p], 16 * i + 16)
                            pe.wait_ge(s_zdve if n % 2 else s_zact, NB * i + n // 2 + 1)
                            for k in range(KT):
                                mm = T.matmul(ps[:, n % AB, 0:WC], xg[:, k, b * P:(b + 1) * P], w[:, p, k, :],
                                              start=(k == 0), stop=(k == KT - 1))
                            mm.then_inc(s_mm, 1)

        names = ("z1 z2 xld t1 qkv scores sm_s sm_m sm_mx sm_neg sm_d es exp den rden prob pt ptc oat "
                 "oatc st atm ro rok kvp stn stats var rs rstd yn silu ysil yt ytc ga gates ya mixa "
                 "mixb mix mixt mixtc wo x1 ssq2 ms2 sq2 r2 h2 x1st h2st keep kdec").split()
        s = {n: sem("b_" + n) for n in names}
        s_bw, s_bt, s_cache, s_stl, s_sto = sem("b_weights"), sem("b_tables"), sem("b_cache"), sem("b_state_in"), sem("b_state_out")
        s_copy, s_samp, s_wb, s_fin = sem("b_cache_copy"), sem("b_sample_tables"), sem("b_wb_wo"), sem("b_final_rows")
        s_zero, s_qm, s_kdm, s_sread, s_supd, s_smm = sem("b_zero"), sem("b_qm"), sem("b_kdm"), sem("b_sread"), sem("b_supd"), sem("b_smm")
        s_vstep, s_qbd, s_tab = sem("b_dve_step"), sem("b_qbd"), sem("b_prompt_tables")

        with ExitStack() as b_:
            Z1 = sb(b_, "Z1", [P, RG])
            Z2 = sb(b_, "Z2", [P, D_IN - RG])
            HO = sb(b_, "HO", [P, D])
            X = sb(b_, "X", [P, D])
            Pr = sb(b_, "Pr", [P, HA, 2 * P])
            PT = sb(b_, "PT", [P, HA, 2, P])
            qaT = sb(b_, "qaT", [P, GRP, P])
            kaT = sb(b_, "kaT", [P, 2, P])
            va = sb(b_, "va", [P, 2, P])
            qbT = sb(b_, "qbT", [P, HB, P])
            kbT = sb(b_, "kbT", [P, HB, P])
            qdT = sb(b_, "qdT", [P, HB, P])
            atm = sb(b_, "atm", [P, HB, P])
            oaT = sb(b_, "oaT", [P, GRP, P])
            yn = sb(b_, "yn", [P, HB, DV])
            yT = sb(b_, "yT", [P, KT, P])
            bg = sb(b_, "bg", [P, 2 * D])
            gf = sb(b_, "gf", [P, D])
            wa = sb(b_, "wa", [P, 4, D])
            sink = sb(b_, "sink", [P, HA])
            mx = sb(b_, "mx", [P, HA])
            ngm = sb(b_, "ngm", [P, HA])
            es = sb(b_, "es", [P, HA])
            rs = sb(b_, "rs", [P, HA])
            stats = sb(b_, "stats", [P, HB, 6])
            mv = sb(b_, "mv", [P, HB, 2])
            sdv = sb(b_, "sdv", [P, HB])
            sm2 = sb(b_, "sm2", [P, 4])
            sink_s = sb(b_, "sink_s", [P, 1])

            a_ = ExitStack()
            kcT = sb(a_, "kcT", [P, DEC_B, WINDOW + DEC_S])
            vc = sb(a_, "vc", [P, DEC_B, P])
            vn = sb(a_, "vn", [DEC_S, DEC_B, P])
            qbd = sb(a_, "qbd", [P, DEC_B, P])
            alibi_s = sb(a_, "alibi_s", [P, WINDOW + DEC_S])
            intra_s = sb(a_, "intra_s", [P, HB, P])
            into_s = sb(a_, "into_s", [P, HB, P])
            out_s = sb(a_, "out_s", [P, DEC_B, HB])
            a_.close()
            alibi = sb(b_, "alibi", [P, HA, 2 * P])
            alibi_c = sb(b_, "alibi_c", [P, HA, P])
            intra = sb(b_, "intra", [P, HB, P])
            into = sb(b_, "into", [P, HB, P])
            outd = sb(b_, "outd", [P, HB])
            kdec = sb(b_, "kdec", [P, HB, DK])
            st = sb(b_, "st", [P, HB, DV])
            c_ = ExitStack()
            st_s = sb(c_, "st_s", [P, HB, DEC_B, DV])
            qm = sb(c_, "qm", [P, HB, DEC_B, P])
            kdm = sb(c_, "kdm", [P, DEC_B, HB, DK])
            c_.close()
            wb = sb(b_, "wb", [P, KT, D])
            wo = sb(b_, "wo", [P, KT, D])

            def z(lo, n):
                return Z1[:, lo:lo + n] if lo < RG else Z2[:, lo - RG:lo - RG + n]

            def load_mixers(sp, blk):
                sp.dma_start(Z1[:], rows(z_d[:, 0:RG], blk)).then_inc(s["z1"], 16)

            def load_gates(sp, blk):
                sp.dma_start(Z2[:], rows(z_d[:, RG:], blk)).then_inc(s["z2"], 16)

            def load_rows(sp, blk):
                sp.dma_start(X[:], rows(t["x"], blk)).then_inc(s["xld"], 16)

            def store_block(g, blk):
                g.wait_ge(s["x1"], blk + 1)
                g.sem_inc(s_pool, 1)
                g.dma_start(rows(x1_d, blk), X[:]).then_inc(s["x1st"], 16)
                g.wait_ge(s["h2"], blk + 1)
                g.sem_inc(s_pool, 1)
                g.dma_start(rows(h2_d, blk), HO[:]).then_inc(s["h2st"], 16)

            def pe_transposes(pe, blk):
                pe.wait_ge(s["z1"], 16 * blk + 16)
                for n, lo in enumerate([QA + P * j for j in range(4)] + [QB + P * j for j in range(4)]
                                       + [KB + P * j for j in range(4)] + [KA]):
                    mm = T.transpose(ps[:, n // 4, (n % 4) * P:(n % 4 + 1) * P], z(lo, P), ident[:])
                mm.then_inc(s["t1"], 1)

            def pe_gated_transposes(pe, blk):
                pe.wait_ge(s["ysil"], blk + 1)
                for k in range(KT):
                    mm = T.transpose(ps[:, 4 + k // 4, (k % 4) * P:(k % 4 + 1) * P], z(RG + P * k, P), ident[:])
                mm.then_inc(s["yt"], 1)

            def pe_branches(pe, blk):
                pe.wait_ge(s["ytc"], blk + 1)
                pe.wait_ge(s["oatc"], blk + 1)
                for n in range(2):
                    for k in range(4):
                        T.matmul(bank(4 + n), oaT[:, k, :], wa[:, k, n * 512:(n + 1) * 512], start=(k == 0), stop=(k == 3))
                for n in range(2):
                    for k in range(KT):
                        mm = T.matmul(bank(6 + n), yT[:, k, :], wb[:, k, n * 512:(n + 1) * 512], start=(k == 0), stop=(k == KT - 1))
                mm.then_inc(s["ya"], 1)

            def pe_mix_transposes(pe, blk):
                pe.wait_ge(s["mix"], blk + 1)
                for k in range(KT):
                    mm = T.transpose(ps[:, 4 + k // 4, (k % 4) * P:(k % 4 + 1) * P], z(GA + P * k, P), ident[:])
                mm.then_inc(s["mixt"], 1)

            def pe_output(pe, blk):
                pe.wait_ge(s["mixtc"], blk + 1)
                for n in range(2):
                    for k in range(KT):
                        mm = T.matmul(bank(6 + n), yT[:, k, :], wo[:, k, n * 512:(n + 1) * 512], start=(k == 0), stop=(k == KT - 1))
                mm.then_inc(s["wo"], 1)

            def pe_scores_b(pe, blk):
                for h in range(HB):
                    mm = T.matmul(ps[:, 6, h * P:(h + 1) * P], kbT[:, h, :], qbT[:, h, :], start=True, stop=True)
                mm.then_inc(s["st"], 1)

            def act_exps(act, blk, width):
                act.wait_ge(s["sm_d"], blk + 1)
                S.activation(es[:], es[:], ACT.Exp).then_inc(s["es"], 1)
                for h in range(HA):
                    e = S.activation(Pr[:, h, 0:width], Pr[:, h, 0:width], ACT.Exp, bias=ngm[:, h:h + 1], accum_out=rs[:, h:h + 1])
                e.then_inc(s["exp"], 1)

            def act_gate(act, blk):
                act.wait_ge(s["z2"], 16 * blk + 16)
                S.activation(z(RG, D), z(RG, D), ACT.Silu).then_inc(s["silu"], 1)

            def act_sigmoids(act, blk):
                act.wait_ge(s["ga"], blk + 1)
                S.activation(z(GA, 2 * D), z(GA, 2 * D), ACT.Sigmoid).then_inc(s["gates"], 1)

            def act_gated(act, blk):
                act.wait_ge(s["yt"], blk + 1)
                S.activation(yT[:].rearrange("p k n -> p (k n)"), bank(4, 2), ACT.Copy).then_inc(s["ytc"], 1)

            def act_mix(act, blk):
                act.wait_ge(s["mixt"], blk + 1)
                S.activation(yT[:].rearrange("p k n -> p (k n)"), bank(4, 2), ACT.Copy).then_inc(s["mixtc"], 1)

            def act_deviation(act, blk):
                act.wait_ge(s["var"], blk + 1)
                S.activation(sdv[:], sdv[:], ACT.Sqrt).then_inc(s["rs"], 1)

            def act_norm2(act, blk):
                act.wait_ge(s["x1"], blk + 1)
                S.activation(HO[:], X[:], ACT.Square, accum_out=sm2[:, 0:1]).then_inc(s["ssq2"], 1)
                act.wait_ge(s["ms2"], blk + 1)
                S.activation(sm2[:, 2:3], sm2[:, 1:2], ACT.Sqrt).then_inc(s["sq2"], 1)

            def dve_softmax(v, blk, width, sinks, step):
                pr = Pr[:, :, 0:width]
                v.wait_ge(s["sm_s"], blk + 1)
                V.tensor_reduce(mx[:], pr, op=ALU.max, axis=AX.X).then_inc(s["sm_m"], 1)
                v.wait_ge(s["sm_m"], blk + 1)
                V.tensor_tensor(mx[:], mx[:], sinks, ALU.max).then_inc(s["sm_mx"], 1)
                v.wait_ge(s["sm_mx"], blk + 1)
                V.tensor_scalar(ngm[:], mx[:], -1.0, None, ALU.mult).then_inc(s["sm_neg"], 1)
                V.tensor_tensor(es[:], sinks, mx[:], ALU.subtract).then_inc(s["sm_d"], 1)

            def dve_probs(v, blk, width):
                pr = Pr[:, :, 0:width]
                v.wait_ge(s["exp"], blk + 1)
                V.tensor_tensor(rs[:], rs[:], es[:], ALU.add).then_inc(s["den"], 1)
                v.wait_ge(s["den"], blk + 1)
                V.reciprocal(rs[:], rs[:]).then_inc(s["rden"], 1)
                v.wait_ge(s["rden"], blk + 1)
                V.tensor_tensor(pr, pr, rs[:].unsqueeze(2).to_broadcast([P, HA, width]), ALU.mult).then_inc(s["prob"], 1)

            def dve_retention_norm(v, blk, b0, step):
                v.wait_ge(s["ro"], blk + 1)
                for h in range(HB):
                    q = V.bn_stats(stats[:, h, :], ps[:, b0 + h // 2, (h % 2) * DV:(h % 2 + 1) * DV])
                step.did(q)
                step.settle()
                v.sem_inc(s["rok"], 1)
                for h in range(HB):
                    q = V.bn_aggr(mv[:, h, :], stats[:, h, :])
                q.then_inc(s["stats"], 1)
                v.wait_ge(s["stats"], blk + 1)
                V.tensor_scalar(sdv[:], mv[:, :, 1], EPS, None, ALU.add).then_inc(s["var"], 1)
                v.wait_ge(s["rs"], blk + 1)
                V.reciprocal(sdv[:], sdv[:]).then_inc(s["rstd"], 1)
                v.wait_ge(s["rstd"], blk + 1)
                for h in range(HB):
                    q = V.tensor_scalar(yn[:, h, :], ps[:, b0 + h // 2, (h % 2) * DV:(h % 2 + 1) * DV],
                                        mv[:, h, 0:1], sdv[:, h:h + 1], ALU.subtract, ALU.mult)
                q.then_inc(s["yn"], 1)

            def dve_gate(v, blk):
                v.wait_ge(s["yn"], blk + 1)
                v.wait_ge(s["silu"], blk + 1)
                V.tensor_tensor(z(RG, D), z(RG, D), yn[:].rearrange("p h n -> p (h n)"), ALU.mult).then_inc(s["ysil"], 1)
                V.tensor_tensor(z(GA, 2 * D), z(GA, 2 * D), bg[:], ALU.add).then_inc(s["ga"], 1)

            def dve_merge(v, blk):
                v.wait_ge(s["gates"], blk + 1)
                v.wait_ge(s["ya"], blk + 1)
                V.tensor_tensor(z(GA, D), z(GA, D), bank(4, 2), ALU.mult).then_inc(s["mixa"], 1)
                V.tensor_tensor(z(GB, D), z(GB, D), bank(6, 2), ALU.mult).then_inc(s["mixb"], 1)
                v.wait_ge(s["mixb"], blk + 1)
                V.tensor_tensor(z(GA, D), z(GA, D), z(GB, D), ALU.add).then_inc(s["mix"], 1)

            def dve_residual(v, blk):
                v.wait_ge(s["wo"], blk + 1)
                v.wait_ge(s["xld"], 16 * blk + 16)
                V.tensor_tensor(X[:], X[:], bank(6, 2), ALU.add).then_inc(s["x1"], 1)

            def dve_norm2(v, blk):
                v.wait_ge(s["ssq2"], blk + 1)
                V.tensor_scalar(sm2[:, 1:2], sm2[:, 0:1], 1.0 / D, EPS, ALU.mult, ALU.add).then_inc(s["ms2"], 1)
                v.wait_ge(s["sq2"], blk + 1)
                V.reciprocal(sm2[:, 3:4], sm2[:, 2:3]).then_inc(s["r2"], 1)
                v.wait_ge(s["r2"], blk + 1)
                V.scalar_tensor_tensor(HO[:], X[:], sm2[:, 3:4], gf[:], ALU.mult, ALU.mult).then_inc(s["h2"], 1)

            with nc.Block() as block:
                @block.sync
                def _(sp):
                    for p in range(2):
                        sp.wait_ge(s_zst[p], 16 * (WT // 2))
                    load_mixers(sp, 0)
                    sp.dma_start(bg[:], t["b_gate"].to_broadcast([P, 2 * D])).then_inc(s_bw, 16)
                    sp.dma_start(gf[:], t["norm_ffn"].to_broadcast([P, D])).then_inc(s_bw, 16)
                    sp.dma_start(sink[:], t["sinks"].to_broadcast([P, HA])).then_inc(s_bw, 16)
                    sp.dma_start(sink_s[:], t["sinks_rows"]).then_inc(s_bw, 16)
                    sp.dma_start(alibi_s[:], t["alibi_s"]).then_inc(s_samp, 16)
                    sp.dma_start(intra_s[:].rearrange("p h n -> p (h n)"), t["intra_s"]).then_inc(s_samp, 16)
                    sp.dma_start(into_s[:].rearrange("p h n -> p (h n)"), t["into_s"]).then_inc(s_samp, 16)
                    sp.dma_start(out_s[:].rearrange("p h n -> p (h n)"), t["out_dec_s"]).then_inc(s_samp, 16)
                    sp.dma_start(kcT[:, :, 0:WINDOW], t["cache_kt"].rearrange("p (b w) -> p b w", b=DEC_B)).then_inc(s_cache, 16)
                    sp.dma_start(vc[:], t["cache_v"].rearrange("(b w) c -> w b c", w=WINDOW)).then_inc(s_cache, 16)
                    sp.dma_start(vn[:], z_d[0:P, VA:VA + P].rearrange("(b n) c -> n b c", n=DEC_S)).then_inc(s_cache, 16)
                    for h in range(HB):
                        sp.dma_start(st_s[:, h], t["state"].rearrange("(b h p) v -> h p b v", h=HB, p=DK)[h]).then_inc(s_stl, 16)
                    load_gates(sp, 0)
                    sp.dma_start(wa[:], t["w_branch_a"].rearrange("(k p) n -> p k n", p=P)).then_inc(s_bw, 16)
                    for src, dst, lo in ((t["cache_k"], o["kc"], KA), (t["cache_v"], o["vc"], VA)):
                        r = dst.rearrange("(b w) c -> b w c", w=WINDOW)
                        sp.dma_start(r[:, 0:WINDOW - DEC_S], src.rearrange("(b w) c -> b w c", w=WINDOW)[:, DEC_S:]).then_inc(s_copy, 16)
                        sp.dma_start(r[:, WINDOW - DEC_S:], z_d[0:P, lo:lo + P].rearrange("(b n) c -> b n c", n=DEC_S)).then_inc(s_copy, 16)
                    for src, dst in ((KA, o["kp"]), (VA, o["vp"])):
                        sp.dma_start(dst, z_d[(NB - 1) * P:, src:src + P]).then_inc(s_copy, 16)
                    for h in range(HB):
                        sp.wait_ge(s_supd, h + 1)
                        sp.dma_start(o["ss"].rearrange("(b h p) v -> h p b v", h=HB, p=DK)[h], st_s[:, h]).then_inc(s_sto, 16)
                    sp.wait_ge(s_sto, 16 * HB)
                    sp.dma_start(wb[:], t["w_branch_b"].rearrange("(k p) n -> p k n", p=P)).then_inc(s_wb, 16)
                    sp.dma_start(wo[:], t["w_out"].rearrange("(k p) n -> p k n", p=P)).then_inc(s_wb, 16)
                    sp.wait_ge(s["oatc"], 1)
                    sp.wait_ge(s["yn"], 1)
                    sp.dma_start(alibi[:].rearrange("p h n -> p (h n)"), t["alibi"]).then_inc(s_tab, 16)
                    sp.dma_start(intra[:].rearrange("p h n -> p (h n)"), t["intra"]).then_inc(s_tab, 16)
                    sp.dma_start(into[:].rearrange("p h n -> p (h n)"), t["into"]).then_inc(s_tab, 16)
                    sp.dma_start(outd[:], t["out_dec"]).then_inc(s_tab, 16)
                    with sp.Fori(1, NB) as blk:
                        sp.wait_ge(s["keep"], blk)
                        sp.wait_ge(s["stn"], blk)
                        load_mixers(sp, blk)
                        sp.wait_ge(s["mixt"], blk)
                        load_gates(sp, blk)
                    sp.wait_ge(s["stn"], NB)
                    sp.dma_start(o["sp"].rearrange("(h p) v -> p h v", p=DK), st[:]).then_inc(s_sto, 16)
                    sp.wait_ge(s_sto, 16 * HB + 16)
                    sp.wait_ge(s_copy, 16 * 6)

                @block.gpsimd
                def _(g):
                    for p in range(2):
                        g.wait_ge(s_zst[p], 16 * (WT // 2))
                        g.sem_inc(s_pool, 1)
                    load_rows(g, 0)
                    with g.Fori(1, NB) as blk:
                        store_block(g, blk - 1)
                        g.wait_ge(s["x1st"], 16 * blk)
                        g.sem_inc(s_pool, 1)
                        g.wait_ge(s["h2st"], 16 * blk)
                        g.sem_inc(s_pool, 1)
                        load_rows(g, blk)
                    store_block(g, NB - 1)
                    g.wait_ge(s["x1st"], 16 * NB)
                    g.wait_ge(s["h2st"], 16 * NB)

                @block.tensor
                def _(pe):
                    pe.wait_ge(s_const, 16)
                    pe_transposes(pe, 0)
                    pe.wait_ge(s_qbd, 1)
                    pe.wait_ge(s["qkv"], 2)
                    for b in range(DEC_B):
                        mm = T.matmul(ps[:, 4 + b // 2, (b % 2) * 144:(b % 2) * 144 + 144], qbd[:, b, :], kcT[:, b, :], start=True, stop=True)
                    mm.then_inc(s["scores"], 1)
                    pe.wait_ge(s["prob"], 1)
                    for b in range(DEC_B):
                        T.transpose(ps[:, b // 4, (b % 4) * P:(b % 4 + 1) * P], Pr[:, b, 0:P], ident[:])
                    for b in range(DEC_B):
                        mm = T.transpose(ps[0:DEC_S, 2 + b // 4, (b % 4) * P:(b % 4 + 1) * P], Pr[:, b, P:P + DEC_S], ident[:])
                    mm.then_inc(s["pt"], 1)
                    pe.wait_ge(s["ptc"], 2)
                    for b in range(DEC_B):
                        for kv in range(KV):
                            d = ps[HD * kv:HD * kv + HD, 4, :].rearrange("p (j t) -> p j t", j=GRP)[:, :, b * DEC_S:(b + 1) * DEC_S]
                            T.matmul(d, vc[:, b, HD * kv:HD * kv + HD], PT[:, b, 0, HD * kv:HD * kv + HD], start=True, stop=False)
                            mm = T.matmul(d, vn[:, b, HD * kv:HD * kv + HD], PT[0:DEC_S, b, 1, HD * kv:HD * kv + HD], start=False, stop=True)
                    mm.then_inc(s["oat"], 1)
                    pe.wait_ge(s["sm_s"], 1)
                    pe_scores_b(pe, 0)
                    pe.wait_ge(s["atm"], 1)
                    pe.wait_ge(s_qm, 1)
                    pe.wait_ge(s_stl, 16 * HB)
                    for h in range(HB):
                        d = ps[:, 6 + h // 2, (h % 2) * DV:(h % 2 + 1) * DV]
                        mm = T.matmul(d, atm[:, h, :], z(VB + h * DV, DV), start=True, stop=False)
                        for b in range(DEC_B):
                            mm = T.matmul(d, qm[:, h, b, :], st_s[:, h, b, :], start=False, stop=(b == DEC_B - 1))
                    mm.then_inc(s["ro"], 1)
                    pe.wait_ge(s_kdm, 1)
                    for h in range(HB):
                        if h:
                            pe.wait_ge(s_supd, h)
                        for b in range(DEC_B):
                            mm = T.matmul(ps[:, b // 2, (b % 2) * DV:(b % 2 + 1) * DV], kdm[:, b, h, :], z(VB + h * DV, DV), start=True, stop=True)
                        mm.then_inc(s_smm, 1)
                    pe.wait_ge(s_supd, HB)
                    pe.wait_ge(s_bw, 16 * 5)
                    with pe.Fori(1, NB) as blk:
                        pe_transposes(pe, blk)
                        pe.wait_ge(s["qkv"], 2 * blk + 2)
                        for kv in range(KV):
                            for j in range(GRP):
                                mm = T.matmul(ps[:, 2 * kv + j // 2, (j % 2) * 256:(j % 2 + 1) * 256], qaT[HD * kv:HD * kv + HD, j, :],
                                              kaT[HD * kv:HD * kv + HD, :, :].rearrange("p s n -> p (s n)"), start=True, stop=True)
                        mm.then_inc(s["scores"], 1)
                        pe_scores_b(pe, blk)
                        pe_gated_transposes(pe, blk - 1)
                        pe.wait_ge(s["atm"], blk + 1)
                        pe.wait_ge(s_wb, 32)
                        pe_branches(pe, blk - 1)
                        pe.wait_ge(s["prob"], blk + 1)
                        for n in range(2 * HA):
                            mm = T.transpose(ps[:, n // 4, (n % 4) * P:(n % 4 + 1) * P], Pr[:, n // 2, (n % 2) * P:(n % 2 + 1) * P], ident[:])
                        mm.then_inc(s["pt"], 1)
                        pe_mix_transposes(pe, blk - 1)
                        pe.wait_ge(s["ptc"], 2 * blk + 2)
                        for kv in range(KV):
                            for j in range(GRP):
                                for c in range(2):
                                    mm = T.matmul(ps[HD * kv:HD * kv + HD, 0, j * P:(j + 1) * P], va[:, c, HD * kv:HD * kv + HD],
                                                  PT[:, GRP * kv + j, c, :], start=(c == 0), stop=(c == 1))
                        mm.then_inc(s["oat"], 1)
                        pe.wait_ge(s["stn"], blk)
                        for h in range(HB):
                            d = ps[:, 2 + h // 2, (h % 2) * DV:(h % 2 + 1) * DV]
                            T.matmul(d, atm[:, h, :], z(VB + h * DV, DV), start=True, stop=False)
                            mm = T.matmul(d, qdT[:, h, :], st[:, h, :], start=False, stop=True)
                        mm.then_inc(s["ro"], 1)
                        pe_output(pe, blk - 1)
                        for h in range(HB):
                            mm = T.matmul(ps[:, 4 + h // 2, (h % 2) * DV:(h % 2 + 1) * DV], kdec[:, h, :], z(VB + h * DV, DV), start=True, stop=True)
                        mm.then_inc(s["kvp"], 1)
                        pe.wait_ge(s["x1"], blk)
                        pe.wait_ge(s["yn"], blk + 1)
                        pe.wait_ge(s["stn"], blk + 1)
                    pe_gated_transposes(pe, NB - 1)
                    pe_branches(pe, NB - 1)
                    pe_mix_transposes(pe, NB - 1)
                    pe_output(pe, NB - 1)

                @block.scalar
                def _(act):
                    act.wait_ge(s["t1"], 1)
                    act.wait_ge(s_cache, 48)
                    S.activation(kcT[:, :, WINDOW:], ps[:, 3, 0:P].rearrange("p (b n) -> p b n", b=DEC_B), ACT.Copy).then_inc(s["qkv"], 1)
                    S.activation(kbT[:].rearrange("p h n -> p (h n)"), bank(2), ACT.Copy).then_inc(s["qkv"], 1)
                    act_exps(act, 0, WINDOW + DEC_S)
                    act.wait_ge(s["pt"], 1)
                    S.activation(PT[:, :, 0, :], bank(0, 2).rearrange("p (b n) -> p b n", b=DEC_B), ACT.Copy).then_inc(s["ptc"], 1)
                    act_deviation(act, 0)
                    with act.Fori(1, NB) as blk:
                        act_gate(act, blk - 1)
                        act.wait_ge(s["t1"], blk + 1)
                        S.activation(qaT[:].rearrange("p h n -> p (h n)"), bank(0), ACT.Copy)
                        S.activation(kbT[:].rearrange("p h n -> p (h n)"), bank(2), ACT.Copy).then_inc(s["qkv"], 1)
                        act_gated(act, blk - 1)
                        act_exps(act, blk, 2 * P)
                        act_sigmoids(act, blk - 1)
                        act.wait_ge(s["pt"], blk + 1)
                        S.activation(PT[:, 0:4].rearrange("p h c n -> p (h c n)"), bank(0, 2), ACT.Copy).then_inc(s["ptc"], 1)
                        act_mix(act, blk - 1)
                        act_deviation(act, blk)
                        act_norm2(act, blk - 1)
                    act_gate(act, NB - 1)
                    act_gated(act, NB - 1)
                    act_sigmoids(act, NB - 1)
                    act_mix(act, NB - 1)
                    act_norm2(act, NB - 1)

                @block.vector
                def _(v):
                    v.wait_ge(s_zst[0], 16 * (WT // 2))
                    v.wait_ge(s_zst[1], 16 * (WT // 2))
                    V.memset(qbd[:], 0.0).then_inc(s_zero, 1)
                    V.memset(qm[:], 0.0).then_inc(s_zero, 1)
                    v.wait_ge(s_zero, 2)
                    v.wait_ge(s["t1"], 1)
                    for kv in range(KV):
                        q = V.tensor_copy(qbd[HD * kv:HD * kv + HD, :, HD * kv:HD * kv + HD].rearrange("p b (j n) -> p j b n", j=GRP),
                                          ps[HD * kv:HD * kv + HD, 0, :].rearrange("p (j b n) -> p j b n", j=GRP, b=DEC_B))
                    V.tensor_copy(qbT[:].rearrange("p h n -> p (h n)"), bank(1)).then_inc(s_qbd, 1)
                    v.wait_ge(s_samp, 64)
                    diag = bass.AP(tensor=qm[:].tensor, offset=qm[:].offset,
                                   ap=[list(qm[:].ap[0]), [DEC_B * P, HB], [P + DEC_S, DEC_B], [1, DEC_S]])
                    V.tensor_tensor(diag, bank(1).rearrange("p (h b n) -> p h b n", h=HB, b=DEC_B),
                                    into_s[:].rearrange("p h (b n) -> p h b n", b=DEC_B), ALU.mult).then_inc(s_qm, 1)
                    v.wait_ge(s["z1"], 16)
                    for b in range(DEC_B):
                        q = V.tensor_tensor(kdm[:, b], z(KB, HB * DK).rearrange("p (h d) -> p h d", h=HB),
                                            out_s[:, b, :].unsqueeze(2).to_broadcast([P, HB, DK]), ALU.mult)
                    q.then_inc(s_kdm, 1)
                    v.wait_ge(s["scores"], 1)
                    v.wait_ge(s_bw, 64)
                    for b in range(DEC_B):
                        q = V.scalar_tensor_tensor(Pr[:, b, 0:144], ps[:, 4 + b // 2, (b % 2) * 144:(b % 2) * 144 + 144],
                                                   HD ** -0.5, alibi_s[:], ALU.mult, ALU.add)
                    q.then_inc(s["sm_s"], 1)
                    dve_softmax(v, 0, 144, sink_s[:].to_broadcast([P, DEC_B]), None)
                    dve_probs(v, 0, 144)
                    v.wait_ge(s["pt"], 1)
                    V.tensor_copy(PT[0:DEC_S, :, 1, :], ps[0:DEC_S, 2:4, :].rearrange("p c (b n) -> p (c b) n", n=P)).then_inc(s["ptc"], 1)
                    v.wait_ge(s["oat"], 1)
                    V.tensor_copy(oaT[:].rearrange("p j n -> p (j n)"), bank(4)).then_inc(s["oatc"], 1)
                    v.wait_ge(s["st"], 1)
                    V.tensor_tensor(atm[:].rearrange("p h n -> p (h n)"), bank(6), intra_s[:].rearrange("p h n -> p (h n)"), ALU.mult).then_inc(s["atm"], 1)
                    dve_retention_norm(v, 0, 6, Steps(v, s_vstep))
                    for h in range(HB):
                        v.wait_ge(s_smm, h + 1)
                        V.scalar_tensor_tensor(st_s[:, h].rearrange("p b n -> p (b n)"), st_s[:, h].rearrange("p b n -> p (b n)"),
                                               math.exp(DEC_S * LOG_DECAY[h]), bank(0, 4), ALU.mult, ALU.add).then_inc(s_supd, 1)
                    v.wait_ge(s_tab, 64)
                    V.memset(alibi_c[:], NEG)
                    V.memset(kaT[:, 0], 0.0)
                    V.memset(va[:, 0], 0.0).then_inc(s["keep"], 1)
                    V.memset(st[:], 0.0).then_inc(s["stn"], 1)
                    with v.Fori(1, NB) as blk:
                        step = Steps(v, s_vstep, 1 + (blk - 1) * DVE_B)
                        dve_gate(v, blk - 1)
                        v.wait_ge(s["z1"], 16 * blk + 16)
                        for h in range(HB):
                            q = V.tensor_scalar(kdec[:, h, :], z(KB + h * DK, DK), outd[:, h:h + 1], None, ALU.mult)
                        q.then_inc(s["kdec"], 1)
                        step.did(V.tensor_copy(va[:, 1], z(VA, P)))
                        v.wait_ge(s["t1"], blk + 1)
                        V.tensor_tensor(qdT[:].rearrange("p h n -> p (h n)"), bank(1), into[:].rearrange("p h n -> p (h n)"), ALU.mult)
                        V.tensor_copy(qbT[:].rearrange("p h n -> p (h n)"), bank(1))
                        V.tensor_copy(kaT[:, 1], ps[:, 3, 0:P]).then_inc(s["qkv"], 1)
                        v.wait_ge(s["scores"], blk + 1)
                        sc = ps[:, 0:4, :].rearrange("p b (h n) -> p (b h) n", h=2)
                        V.scalar_tensor_tensor(Pr[:, :, P:], sc[:, :, P:], HD ** -0.5, alibi[:, :, P:], ALU.mult, ALU.add)
                        V.scalar_tensor_tensor(Pr[:, :, 0:P], sc[:, :, 0:P], HD ** -0.5, alibi_c[:], ALU.mult, ALU.add).then_inc(s["sm_s"], 1)
                        v.wait_ge(s["st"], blk + 1)
                        V.tensor_tensor(atm[:].rearrange("p h n -> p (h n)"), bank(6), intra[:].rearrange("p h n -> p (h n)"), ALU.mult).then_inc(s["atm"], 1)
                        dve_softmax(v, blk, 2 * P, sink[:], step)
                        dve_probs(v, blk, 2 * P)
                        v.wait_ge(s["pt"], blk + 1)
                        V.tensor_copy(PT[:, 4:8].rearrange("p h c n -> p (h c n)"), bank(2, 2)).then_inc(s["ptc"], 1)
                        dve_merge(v, blk - 1)
                        v.wait_ge(s["oat"], blk + 1)
                        V.tensor_copy(oaT[:].rearrange("p j n -> p (j n)"), bank(0)).then_inc(s["oatc"], 1)
                        V.tensor_copy(kaT[:, 0], kaT[:, 1])
                        V.tensor_copy(va[:, 0], va[:, 1])
                        V.tensor_copy(alibi_c[:], alibi[:, :, 0:P]).then_inc(s["keep"], 1)
                        dve_retention_norm(v, blk, 2, step)
                        dve_residual(v, blk - 1)
                        v.wait_ge(s["kvp"], blk)
                        for h in range(HB):
                            q = V.scalar_tensor_tensor(st[:, h, :], st[:, h, :], math.exp(P * LOG_DECAY[h]),
                                                       ps[:, 4 + h // 2, (h % 2) * DV:(h % 2 + 1) * DV], ALU.mult, ALU.add)
                        q.then_inc(s["stn"], 1)
                        dve_norm2(v, blk - 1)
                        assert step.n == DVE_B, step.n
                    dve_gate(v, NB - 1)
                    dve_merge(v, NB - 1)
                    dve_residual(v, NB - 1)
                    dve_norm2(v, NB - 1)

        c = {n: sem("c_" + n) for n in "hld ht hcp htc q qc qt qtc sc scc v1 cand b2 ab abf idxf idx gd ge gsum gr gate".split()}
        d = {n: sem("d_" + n) for n in "x1 nf freed gelu act wgt accz y ssq ms sq r yo yst ixl ixd pool gtc".split()}
        s_cw, s_cgate = sem("c_weights"), sem("c_carry")
        s_ring = [sem(f"d_ring{i}") for i in range(RING)]
        UG = NK // PH
        ORDER = [("u", 0)] + [x for g in range(1, PH) for x in (("u", g), ("v", g - 1))] + [("v", PH - 1)]
        USES = 2 * NK // RING
        with ExitStack() as c_:
            wq = sb(c_, "wq", [P, KT, PH * 256])
            kt = sb(c_, "kt", [P, 2, NKEY])
            io = sb(c_, "io", [P, TOPK])
            H = sb(c_, "H", [P, D])
            hT = sb(c_, "hT", [P, KT, P])
            Q = sb(c_, "Q", [P, 16, P])
            qT = sb(c_, "qT", [P, 16, P])
            SC = sb(c_, "SC", [P, 16, NKEY])
            VV = sb(c_, "VV", [P, 16, TOPK])
            II = sb(c_, "II", [P, 16, TOPK], u32)
            IF = sb(c_, "IF", [P, 16, TOPK])
            CA = sb(c_, "CA", [P, PH, TOPK * TOPK])
            BV = sb(c_, "BV", [P, PH, TOPK])
            BP = sb(c_, "BP", [P, PH, TOPK], u32)
            AU = sb(c_, "AU", [P, 2, NK], u32)
            AF = sb(c_, "AF", [P, 2, NK])
            I12 = sb(c_, "I12", [P, 2, NK])
            IX = sb(c_, "IX", [P, NK], u32)
            GT = sb(c_, "GT", [P, PH, TOPK])
            GS = sb(c_, "GS", [P, PH])
            ring = sb(c_, "ring", [P, RING, D])
            X1 = sb(c_, "X1", [P, D])
            H2 = sb(c_, "H2", [P, D])
            IXD = sb(c_, "IXD", [P, NK], u32)
            GD = sb(c_, "GD", [P, NK])
            DOT = sb(c_, "DOT", [P, NK])
            GE = sb(c_, "GE", [P, NK])
            WG = sb(c_, "WG", [P, NK])
            ACC = sb(c_, "ACC", [P, 2, D])
            nf = sb(c_, "nf", [P, D])
            m4 = sb(c_, "m4", [P, 4])

            def pe_keys(pe, blk):
                pe.wait_ge(c["hld"], 16 * blk + 16)
                pe.wait_ge(c["v1"], blk + 1)
                for k in range(KT):
                    mm = T.transpose(ps[:, k // 4, (k % 4) * P:(k % 4 + 1) * P], H[:, k * P:(k + 1) * P], ident[:])
                mm.then_inc(c["ht"], 1)
                pe.wait_ge(c["htc"], blk + 1)
                for n in range(4):
                    for k in range(KT):
                        mm = T.matmul(bank(4 + n), hT[:, k, :], wq[:, k, n * 512:(n + 1) * 512], start=(k == 0), stop=(k == KT - 1))
                    mm.then_inc(c["q"], 1)
                pe.wait_ge(c["qc"], 2 * blk + 2)
                for n in range(16):
                    mm = T.transpose(ps[:, n // 4, (n % 4) * P:(n % 4 + 1) * P], Q[:, n, :], ident[:])
                mm.then_inc(c["qt"], 1)
                pe.wait_ge(c["qtc"], 2 * blk + 2)
                for n in range(16):
                    mm = T.matmul(ps[:, 4 + n // 4, (n % 4) * P:(n % 4 + 1) * P], qT[:, n, :], kt[:, n % 2, :], start=True, stop=True)
                mm.then_inc(c["sc"], 1)

            def act_keys_first(act, blk):
                act.wait_ge(c["ht"], blk + 1)
                S.activation(hT[:].rearrange("p k n -> p (k n)"), bank(0, 2), ACT.Copy).then_inc(c["htc"], 1)
                act.wait_ge(c["q"], 4 * blk + 2)
                S.activation(Q[:, 0:8].rearrange("p k n -> p (k n)"), bank(4, 2), ACT.Copy).then_inc(c["qc"], 1)

            def act_keys_second(act, blk):
                act.wait_ge(c["q"], 4 * blk + 4)
                S.activation(Q[:, 8:16].rearrange("p k n -> p (k n)"), bank(6, 2), ACT.Copy).then_inc(c["qc"], 1)
                act.wait_ge(c["qt"], blk + 1)
                for i in range(2):
                    S.activation(qT[:, 8 * i:8 * i + 8].rearrange("p k n -> p (k n)"), bank(2 * i, 2), ACT.Copy).then_inc(c["qtc"], 1)
                act.wait_ge(c["sc"], blk + 1)
                act.wait_ge(c["scc"], blk + 1)
                S.activation(SC[:].rearrange("p k n -> p (k n)"), bank(4, 4), ACT.Copy).then_inc(c["v1"], 1)

            def act_gates(act, blk):
                act.wait_ge(c["gd"], blk + 1)
                S.activation(GT[:], GT[:], ACT.Exp).then_inc(c["ge"], 1)

            def act_gelu(act, blk, grp):
                act.wait_ge(d["act"], PH * blk + grp + 1)
                cols = slice(grp * UG, (grp + 1) * UG)
                S.activation(GE[:, cols], DOT[:, cols], ACT.Gelu_apprx_tanh).then_inc(d["gelu"], 1)

            def act_norm(act, blk):
                act.wait_ge(d["y"], blk + 1)
                S.activation(ACC[:, 1], ACC[:, 0], ACT.Square, accum_out=m4[:, 0:1]).then_inc(d["ssq"], 1)
                act.wait_ge(d["ms"], blk + 1)
                S.activation(m4[:, 2:3], m4[:, 1:2], ACT.Sqrt).then_inc(d["sq"], 1)

            def pool_gathers(g, blk):
                g.wait_ge(d["ixd"], blk + 1)
                g.sem_inc(d["pool"], 1)
                for n in range(2 * NK):
                    kind, grp = ORDER[n // UG]
                    if n % 4 == 0:
                        g.wait_ge(d["freed"], 2 * NK * blk + n + 4)
                        g.sem_inc(d["pool"], 1)
                    if (kind, n % UG) == ("u", 0) and grp == PH - 1:
                        g.wait_ge(d["ixl"], blk + 1)
                        g.sem_inc(d["pool"], 1)
                    k = grp * UG + n % UG
                    gather = g.indirect_dma_start(ring[:, n % RING, :], None, t["peer_u"] if kind == "u" else t["peer_v"],
                                                  bass.IndirectOffsetOnAxis(ap=IXD[:, k:k + 1], axis=0))
                    gather.then_inc(s_ring[n % RING], 16)

            def carry(v):
                v.sem_inc(s_cgate, 1)

            def dve_maxima(vals, src, lo, n, step):
                for i in range(n):
                    q = V.max(vals[:, i, lo:lo + 8], src[:, i, :])
                step.did(q)

            def dve_places(pos, vals, src, lo, n):
                for i in range(n):
                    q = V.max_index(pos[:, i, lo:lo + 8], vals[:, i, lo:lo + 8], src[:, i, :])
                return q

            def dve_replace(vals, src, n, step):
                for i in range(n):
                    q = V.match_replace(src[:, i, :], vals[:, i, 0:8], src[:, i, :], LOW)
                step.did(q)

            PARTS = 20

            def dve_keys(part, v, blk, step):
                if part == 0:
                    v.wait_ge(c["v1"], blk + 2)
                elif part in (6, 11):
                    v.wait_ge(c["cand"] if part == 6 else c["b2"], blk + 1)
                elif part == 5:
                    v.wait_ge(c["scc"], blk + 2)
                elif part == 12:
                    v.wait_ge(c["abf"], blk + 1)
                elif part != 19:
                    step.settle()
                if part < 11:
                    carry(v)
                oh = CA[:].rearrange("p h (k i) -> p (h k) i", i=TOPK)
                oh4 = CA[:].rearrange("p h (k i) -> p h k i", i=TOPK)
                if part in (0, 3):
                    dve_maxima(VV, SC, 0 if part == 0 else 8, 16, step)
                elif part == 1:
                    step.did(dve_places(II, VV, SC, 0, 16))
                elif part == 2:
                    dve_replace(VV, SC, 16, step)
                elif part == 4:
                    dve_places(II, VV, SC, 8, 16).then_inc(c["scc"], 1)
                elif part == 5:
                    step.did(V.tensor_copy(IF[:], II[:]))
                    V.tensor_tensor(CA[:].rearrange("p h (i j) -> p h i j", i=TOPK),
                                    VV[:, 0::2, :].unsqueeze(3).to_broadcast([P, PH, TOPK, TOPK]),
                                    VV[:, 1::2, :].unsqueeze(2).to_broadcast([P, PH, TOPK, TOPK]), ALU.add).then_inc(c["cand"], 1)
                elif part in (6, 9):
                    dve_maxima(BV, CA, 0 if part == 6 else 8, PH, step)
                elif part == 7:
                    step.did(dve_places(BP, BV, CA, 0, PH))
                elif part == 8:
                    dve_replace(BV, CA, PH, step)
                elif part == 10:
                    dve_places(BP, BV, CA, 8, PH).then_inc(c["b2"], 1)
                elif part == 11:
                    v.wait_ge(d["gtc"], blk + 1)
                    V.tensor_tensor(GT[:], BV[:], BV[:, :, 0:1].to_broadcast([P, PH, TOPK]), ALU.subtract).then_inc(c["gd"], 1)
                    bp = BP[:].rearrange("p h k -> p (h k)")
                    V.tensor_scalar(AU[:, 0], bp, 4, None, ALU.logical_shift_right)
                    V.tensor_scalar(AU[:, 1], bp, 15, None, ALU.bitwise_and).then_inc(c["ab"], 1)
                    v.wait_ge(c["ab"], blk + 1)
                    V.tensor_copy(AF[:], AU[:]).then_inc(c["abf"], 1)
                elif part in (12, 15):
                    step.did(V.tensor_tensor(oh, AF[:, (part - 12) // 3, :].unsqueeze(2).to_broadcast([P, NK, TOPK]),
                                             io[:].unsqueeze(1).to_broadcast([P, NK, TOPK]), ALU.is_equal))
                elif part in (13, 16):
                    step.did(V.tensor_tensor(oh4, oh4, IF[:, (part - 13) // 3::2, :].unsqueeze(2).to_broadcast([P, PH, TOPK, TOPK]), ALU.mult))
                elif part in (14, 17):
                    step.did(V.tensor_reduce(I12[:, (part - 14) // 3, :], oh, op=ALU.add, axis=AX.X))
                elif part == 18:
                    V.scalar_tensor_tensor(I12[:, 0, :], I12[:, 0, :], float(NKEY), I12[:, 1, :], ALU.mult, ALU.add).then_inc(c["idxf"], 1)
                    v.wait_ge(c["idxf"], blk + 1)
                    V.tensor_copy(IX[:], I12[:, 0, :]).then_inc(c["idx"], 1)
                elif part == 19:
                    v.wait_ge(c["ge"], blk + 1)
                    V.tensor_reduce(GS[:], GT[:], op=ALU.add, axis=AX.X).then_inc(c["gsum"], 1)
                    v.wait_ge(c["gsum"], blk + 1)
                    V.reciprocal(GS[:], GS[:]).then_inc(c["gr"], 1)
                    v.wait_ge(c["gr"], blk + 1)
                    V.tensor_tensor(GT[:], GT[:], GS[:].unsqueeze(2).to_broadcast([P, PH, TOPK]), ALU.mult).then_inc(c["gate"], 1)

            def dve_hand_over(v, blk):
                v.wait_ge(c["hld"], 16 * blk + 16)
                V.tensor_copy(H2[:], H[:]).then_inc(c["hcp"], 1)
                v.wait_ge(c["gate"], blk + 1)
                V.tensor_copy(GD[:], GT[:].rearrange("p h k -> p (h k)")).then_inc(d["gtc"], 1)

            def dve_hand_over_places(v, blk):
                v.wait_ge(c["idx"], blk + 1)
                V.tensor_copy(IXD[:, 0:NK - UG], IX[:, 0:NK - UG]).then_inc(d["ixd"], 1)

            def dve_hand_over_last_places(v):
                V.tensor_copy(IXD[:, NK - UG:], IX[:, NK - UG:]).then_inc(d["ixl"], 1)

            FIRST_PART = 7

            def dve_experts(v, blk, more):
                if more:
                    step = Steps(v, s_vstep, STEPS_C + DVE_C * (blk + 1))
                v.wait_ge(c["hcp"], blk + 1)
                v.wait_ge(d["gtc"], blk + 2)
                for n in range(2 * NK):
                    kind, grp = ORDER[n // UG]
                    k = grp * UG + n % UG
                    if more and n % (UG // 2) == 0:
                        part = n // (UG // 2) - FIRST_PART
                        if 0 <= part < PARTS:
                            dve_keys(part, v, blk + 1, step)
                    if kind == "v" and n % UG == 0:
                        cols = slice(grp * UG, (grp + 1) * UG)
                        v.wait_ge(d["gelu"], PH * blk + grp + 1)
                        V.tensor_tensor(WG[:, cols], GE[:, cols], GD[:, cols], ALU.mult).then_inc(d["wgt"], 1)
                        v.wait_ge(d["wgt"], PH * blk + grp + 1)
                        if more and grp == PH - 1:
                            dve_hand_over(v, blk + 1)
                    if more and n == 2 * NK - UG // 2:
                        dve_hand_over_places(v, blk + 1)
                    row = ring[:, n % RING, :]
                    v.wait_ge(s_ring[n % RING], USES * 16 * blk + 16 * (n // RING + 1))
                    if kind == "u":
                        V.tensor_tensor_reduce(out=row, in0=row, in1=H2[:], scale=1.0, scalar=0.0, op0=ALU.mult,
                                               op1=ALU.add, accum_out=DOT[:, k:k + 1]).then_inc(d["freed"], 1)
                        if n % UG == UG - 1:
                            v.wait_ge(d["freed"], 2 * NK * blk + RING + n + 1)
                            v.sem_inc(d["act"], 1)
                    elif k < 2:
                        V.tensor_scalar(ACC[:, k], row, WG[:, k:k + 1], None, ALU.mult).then_inc(d["freed"], 1)
                    else:
                        v.wait_ge(d["freed"], 2 * NK * blk + RING + n - 1)
                        V.scalar_tensor_tensor(ACC[:, k % 2], row, WG[:, k:k + 1], ACC[:, k % 2], ALU.mult, ALU.add).then_inc(d["freed"], 1)
                if more:
                    dve_hand_over_last_places(v)
                v.wait_ge(d["freed"], 2 * NK * blk + RING + 2 * NK)
                V.tensor_tensor(ACC[:, 0], ACC[:, 0], ACC[:, 1], ALU.add).then_inc(d["accz"], 1)
                v.wait_ge(d["accz"], blk + 1)
                v.wait_ge(d["x1"], 16 * blk + 16)
                V.tensor_tensor(ACC[:, 0], ACC[:, 0], X1[:], ALU.add).then_inc(d["y"], 1)
                v.wait_ge(d["ssq"], blk + 1)
                V.tensor_scalar(m4[:, 1:2], m4[:, 0:1], 1.0 / D, EPS, ALU.mult, ALU.add).then_inc(d["ms"], 1)
                v.wait_ge(d["sq"], blk + 1)
                V.reciprocal(m4[:, 3:4], m4[:, 2:3]).then_inc(d["r"], 1)
                v.wait_ge(d["r"], blk + 1)
                V.scalar_tensor_tensor(X1[:], ACC[:, 0], m4[:, 3:4], nf[:], ALU.mult, ALU.mult).then_inc(d["yo"], 1)

            with nc.Block() as block:
                @block.sync
                def _(sp):
                    sp.dma_start(H[:], rows(h2_d, 0)).then_inc(c["hld"], 16)
                    for k in range(KT):
                        sp.dma_start(wq[:, k], t["peer_w_q"][k * P:(k + 1) * P, :]).then_inc(s_cw, 16)
                    sp.dma_start(kt[:, 0], t["sub_k1t"]).then_inc(s_cw, 16)
                    sp.dma_start(kt[:, 1], t["sub_k2t"]).then_inc(s_cw, 16)
                    sp.dma_start(io[:], t["iota16"]).then_inc(s_cw, 16)
                    sp.dma_start(nf[:], t["norm_final"].to_broadcast([P, D])).then_inc(d["nf"], 16)
                    sp.dma_start(X1[:], rows(x1_d, 0)).then_inc(d["x1"], 16)
                    with sp.Fori(1, NB) as blk:
                        sp.wait_ge(c["ht"], blk)
                        sp.wait_ge(c["hcp"], blk)
                        sp.dma_start(H[:], rows(h2_d, blk)).then_inc(c["hld"], 16)
                        sp.wait_ge(d["yo"], blk)
                        sp.dma_start(rows(o["y"], blk - 1), X1[:]).then_inc(d["yst"], 16)
                        sp.wait_ge(d["yst"], 16 * blk)
                        sp.dma_start(X1[:], rows(x1_d, blk)).then_inc(d["x1"], 16)
                    sp.wait_ge(d["yo"], NB)
                    sp.dma_start(rows(o["y"], NB - 1), X1[:]).then_inc(d["yst"], 16)
                    sp.wait_ge(d["yst"], 16 * NB)

                @block.tensor
                def _(pe):
                    pe.wait_ge(s_cw, 16 * (KT + 3))
                    with pe.Fori(0, NB) as blk:
                        pe_keys(pe, blk)

                @block.scalar
                def _(act):
                    act.sem_inc(c["v1"], 1)
                    act_keys_first(act, 0)
                    act_keys_second(act, 0)
                    act_gates(act, 0)
                    with act.Fori(0, NB - 1) as blk:
                        act_keys_first(act, blk + 1)
                        act_gelu(act, blk, 0)
                        act_keys_second(act, blk + 1)
                        for grp in range(1, 5):
                            act_gelu(act, blk, grp)
                        act_gates(act, blk + 1)
                        for grp in range(5, PH):
                            act_gelu(act, blk, grp)
                        act_norm(act, blk)
                    for grp in range(PH):
                        act_gelu(act, NB - 1, grp)
                    act_norm(act, NB - 1)

                @block.vector
                def _(v):
                    v.sem_inc(c["scc"], 1)
                    v.sem_inc(d["gtc"], 1)
                    v.sem_inc(d["freed"], RING)
                    v.wait_ge(s_cw, 16 * (KT + 3))
                    v.wait_ge(d["nf"], 16)
                    step = Steps(v, s_vstep, STEPS_C)
                    for part in range(PARTS):
                        dve_keys(part, v, 0, step)
                    assert step.n == DVE_C, step.n
                    dve_hand_over(v, 0)
                    dve_hand_over_places(v, 0)
                    dve_hand_over_last_places(v)
                    with v.Fori(0, NB - 1) as blk:
                        dve_experts(v, blk, True)
                    dve_experts(v, NB - 1, False)

                @block.gpsimd
                def _(g):
                    with g.Fori(0, NB) as blk:
                        pool_gathers(g, blk)


def kernel(**inputs):
    import concourse.bacc as bacc
    from concourse.bass_utils import run_bass_kernel_spmd

    i = {n: np.asarray(a) for n, a in inputs.items()}
    x = np.concatenate([i["x_sample"].reshape(P, D), i["x_prompt"].reshape(SEQ, D)], 0)
    pair = [h for j in range(GRP) for h in (j, GRP + j)]
    w_in = i["w_in"][0]
    w_in = np.concatenate([w_in[:, :HA * HD].reshape(D, HA, HD)[:, pair].reshape(D, HA * HD), w_in[:, HA * HD:]], 1)
    sinks = i["attn_sinks"][0]
    a = {
        "x": x, "x_t": x.T,
        "w_in": w_in.reshape(KT, P, WT, WC).transpose(2, 1, 0, 3).reshape(WT * P, KT * WC),
        "norm_mix": i["norm_mix"][0].reshape(KT, P).T,
        "b_gate": i["b_gate"], "norm_ffn": i["norm_ffn"], "norm_final": i["norm_final"].reshape(1, D),
        "sinks": sinks.reshape(1, HA), "sinks_rows": np.repeat(sinks, DEC_S).reshape(P, 1),
        "cache_kt": i["cache_swa_k"].reshape(DEC_B * WINDOW, P).T,
        "cache_k": i["cache_swa_k"].reshape(DEC_B * WINDOW, P), "cache_v": i["cache_swa_v"].reshape(DEC_B * WINDOW, P),
        "state": i["state_ret"].reshape(DEC_B * HB * DK, DV),
        "w_branch_a": i["w_branch_a"][0].reshape(HA, HD, D)[pair].reshape(HA * HD, D),
        "w_branch_b": i["w_branch_b"][0], "w_out": i["w_out"][0],
        "peer_w_q": i["peer_w_q"][0], "sub_k1t": i["peer_sub_k1"][0].T, "sub_k2t": i["peer_sub_k2"][0].T,
        "peer_u": i["peer_u"][0], "peer_v": i["peer_v"][0],
    } | shape_tables()
    outs = {"y": (NB * P, D), "kp": (WINDOW, P), "vp": (WINDOW, P), "sp": (HB * DK, DV),
            "kc": (DEC_B * WINDOW, P), "vc": (DEC_B * WINDOW, P), "ss": (DEC_B * HB * DK, DV)}
    nc = bacc.Bacc("TRN2", target_bir_lowering=False, num_devices=1)
    arrays, t, o = {}, {}, {}
    for n, v in a.items():
        arrays[f"in_{n}"] = np.ascontiguousarray(v)
        t[n] = nc.dram_tensor(f"in_{n}", v.shape, mybir.dt.from_np(v.dtype), kind="ExternalInput").ap()
    for n, shape in outs.items():
        o[n] = nc.dram_tensor(f"out_{n}", shape, f32, kind="ExternalOutput").ap()
    trunk_kernel(nc, t, o)
    r = run_bass_kernel_spmd(nc, [arrays], core_ids=[0]).results[0]
    g = {n: r[f"out_{n}"] for n in outs}
    return (g["y"][P:].reshape(1, SEQ, D), g["y"][:P].reshape(DEC_B, DEC_S, D),
            g["kp"].reshape(1, 1, WINDOW, KV, HD), g["vp"].reshape(1, 1, WINDOW, KV, HD), g["sp"].reshape(1, 1, HB, DK, DV),
            g["kc"].reshape(1, DEC_B, WINDOW, KV, HD), g["vc"].reshape(1, DEC_B, WINDOW, KV, HD), g["ss"].reshape(1, DEC_B, HB, DK, DV))
```

```python
import math
from contextlib import ExitStack

import concourse.bass as bass
import numpy as np
from concourse import mybir

P = 128
D = 1024
KT = D // P
SEQ, DEC_B, DEC_S = 1024, 8, 16
NB = 1 + SEQ // P
CHUNK, WINDOW, EPS, NEG = 64, 128, 1e-6, -1e30
HA, KV, GRP, HD = 8, 2, 4, 64
HB, DK, DV = 4, 128, 256
QA, KA, VA, QB, KB, VB, RG, GA, GB, D_IN = (0, 512, 640, 768, 1280, 1792, 2816, 3840, 4864, 5888)
WT = 16
WC = D_IN // WT
NKEY, PH, TOPK = 128, 8, 16
NEXP = NKEY * NKEY
NK = PH * TOPK
RING = 16
LOW = -3.0e38
LOG_DECAY = [math.log1p(-(2.0 ** (-5.0 - h))) for h in range(HB)]

f32 = mybir.dt.float32
u32 = mybir.dt.uint32
ALU = mybir.AluOpType
ACT = mybir.ActivationFunctionType
AX = mybir.AxisListType


def shape_tables():
    q = np.arange(P)[:, None].astype(np.float64)
    slopes = 2.0 ** -(np.arange(HA) + 1.0)
    k = np.arange(2 * P)[None, :]
    dist = np.abs(P + q - k)
    seen = ((q < CHUNK) & (k < 3 * CHUNK)) | ((q >= CHUNK) & (k >= CHUNK))
    alibi = np.where(seen[:, None, :], -slopes[None, :, None] * dist[:, None, :], NEG)
    row = np.arange(P)
    ks = np.arange(WINDOW + DEC_S)[None, :]
    alibi_s = -slopes[row // DEC_S][:, None] * np.abs(WINDOW + (row % DEC_S)[:, None] - ks)
    lg = np.array(LOG_DECAY)
    m, n = np.arange(P)[:, None], np.arange(P)[None, :]
    intra = np.stack([np.where(n >= m, np.exp((n - m) * g), 0.0) for g in lg], 1) * DK ** -0.5
    same = (m // DEC_S) == (n // DEC_S)
    intra_s = intra * same[:, None, :]
    into = np.exp((np.arange(P) + 1.0)[None, :] * lg[:, None])
    into_s = np.exp((np.arange(P) % DEC_S + 1.0)[None, :] * lg[:, None])
    out = np.exp((P - 1.0 - np.arange(P))[:, None] * lg[None, :]) * DK ** -0.5
    out_s = np.exp((DEC_S - 1.0 - np.arange(P) % DEC_S)[:, None] * lg[None, :]) * DK ** -0.5
    out_s = out_s[:, None, :] * (np.arange(P)[:, None, None] // DEC_S == np.arange(DEC_B)[None, :, None])
    t = {
        "ident": np.eye(P), "alibi": alibi, "alibi_s": alibi_s, "intra": intra, "intra_s": intra_s,
        "into": np.broadcast_to(into[None], (P, HB, P)), "into_s": np.broadcast_to(into_s[None], (P, HB, P)),
        "out_dec": out, "out_dec_s": out_s, "iota16": np.broadcast_to(np.arange(TOPK)[None, :], (P, TOPK)),
    }
    return {n: np.ascontiguousarray(a.reshape(P, -1).astype(np.float32)) for n, a in t.items()}


class Steps:

    def __init__(self, eng, sem, base=0):
        self.eng, self.sem, self.base, self.n = eng, sem, base, 0

    def did(self, ins):
        ins.then_inc(self.sem, 1)
        self.n += 1

    def settle(self):
        self.eng.wait_ge(self.sem, self.base + self.n)


DVE_B = 2
DVE_C = 15
STEPS_C = 1 + (NB - 1) * DVE_B


def trunk_kernel(nc, t, o):
    V, S, G, T = nc.vector, nc.scalar, nc.gpsimd, nc.tensor
    ctx = ExitStack()
    with ctx:
        def sb(stack, name, shape, dt=f32):
            return stack.enter_context(nc.sbuf_tensor(name, shape, dt))

        def sem(name):
            return ctx.enter_context(nc.semaphore(name))

        def dram(name, shape, dt=f32):
            return nc.dram_tensor(name, shape, dt, kind="Internal").ap()

        z_d = dram("z_d", (NB * P, D_IN))
        x1_d = dram("x1_d", (NB * P, D))
        h2_d = dram("h2_d", (NB * P, D))
        idx_d = dram("idx_d", (NB * P, NK), u32)
        gate_d = dram("gate_d", (NB * P, NK))

        ps = ctx.enter_context(nc.psum_tensor("ps", [P, 8, 512], f32))
        ident = sb(ctx, "ident", [P, P])
        s_const = sem("s_const")

        def bank(b, n=1):
            return ps[:, b:b + n, :].rearrange("p b n -> p (b n)")

        def rows(ap, blk):
            return ap[bass.ds(blk * P, P), :] if not isinstance(blk, int) else ap[blk * P:(blk + 1) * P, :]

        s_xt, s_x, s_g, s_kv = sem("s_xt"), sem("s_x"), sem("s_g"), sem("s_kv")
        s_w = [sem(f"s_w{i}") for i in range(2)]
        s_ssq, s_ms, s_sq, s_rstd, s_xg = sem("s_ssq"), sem("s_ms"), sem("s_sq"), sem("s_rstd"), sem("s_xg")
        s_mm, s_zact = sem("s_mm"), sem("s_zact")
        s_zst = [sem(f"s_zst{i}") for i in range(2)]
        s_pool = sem("s_pool")
        AB = 8
        rstd = sb(ctx, "rstd", [P, NB])
        gm = sb(ctx, "gm", [P, KT])
        first = ctx.enter_context(ExitStack())
        Z = sb(first, "Z0", [P, D_IN])

        with ExitStack() as a:
            xg0 = sb(a, "xg0", [P, KT, P])
            xn = sb(a, "xn", [P, NB, D])
            w0 = sb(a, "w0", [P, 2, 2, KT, WC])
            ssq = sb(a, "ssq", [P, NB])
            junk = sb(a, "junk", [P, 2, D])
            with nc.Block() as block:
                @block.sync
                def _(sp):
                    sp.dma_start(gm[:], t["norm_mix"]).then_inc(s_g, 16)
                    sp.dma_start(xg0[:], t["x_t"][:, 0:P].rearrange("(k p) n -> p k n", p=P)).then_inc(s_xt, 16)
                    for p in range(WT // 2):
                        if p == 1:
                            sp.dma_start(xn[:], t["x"].rearrange("(b p) d -> p b d", p=P)).then_inc(s_x, 16)
                            sp.dma_start(ident[:], t["ident"]).then_inc(s_const, 16)
                        if p >= 2:
                            sp.wait_ge(s_mm, 2 * (p - 1))
                        sp.dma_start(w0[:, p % 2].rearrange("p j k c -> p j (k c)"),
                                     t["w_in"][2 * p * P:(2 * p + 2) * P, :].rearrange("(j p) c -> p j c", p=P)).then_inc(s_w[p % 2], 16)

                @block.scalar
                def _(act):
                    act.wait_ge(s_x, 16)
                    for b in range(NB):
                        if b >= 2:
                            act.wait_ge(s_ssq, b - 1)
                        S.activation(junk[:, b % 2, :], xn[:, b, :], ACT.Square, accum_out=ssq[:, b:b + 1]).then_inc(s_ssq, 1)
                    act.wait_ge(s_ms, 1)
                    S.activation(rstd[:], ssq[:], ACT.Sqrt).then_inc(s_sq, 1)
                    act.wait_ge(s_rstd, 1)
                    for n in range(WT):
                        act.wait_ge(s_mm, n + 1)
                        S.activation(Z[:, n * WC:(n + 1) * WC], ps[:, n % AB, 0:WC], ACT.Copy, scale=rstd[:, 0:1]).then_inc(s_zact, 1)

                @block.vector
                def _(v):
                    v.wait_ge(s_g, 16)
                    v.wait_ge(s_xt, 16)
                    for k in range(KT):
                        V.tensor_scalar(xg0[:, k, :], xg0[:, k, :], gm[:, k:k + 1], None, ALU.mult).then_inc(s_xg, 1)
                    v.wait_ge(s_ssq, NB)
                    V.tensor_scalar(ssq[:], ssq[:], 1.0 / D, EPS, ALU.mult, ALU.add).then_inc(s_ms, 1)
                    v.wait_ge(s_sq, 1)
                    V.reciprocal(rstd[:], rstd[:]).then_inc(s_rstd, 1)

                @block.tensor
                def _(pe):
                    pe.wait_ge(s_xg, KT)
                    for n in range(WT):
                        p = n // 2
                        if n % 2 == 0:
                            pe.wait_ge(s_w[p % 2], 16 * (p // 2 + 1))
                        if n >= AB:
                            pe.wait_ge(s_zact, n - AB + 1)
                        for k in range(KT):
                            mm = T.matmul(ps[:, n % AB, 0:WC], xg0[:, k, :], w0[:, p % 2, n % 2, k, :],
                                          start=(k == 0), stop=(k == KT - 1))
                        mm.then_inc(s_mm, 1)

        names = ("z1 z1b z2 xld t1 qkv scores sm_s sm_m sm_mx sm_neg sm_d es exp den rden prob pt ptc oat "
                 "oatc st atm ro rok kvp stn stats var rs rstd yn silu ysil yt ytc ga gates ya mixa "
                 "mixb mix mixt mixtc wo x1 ssq2 ms2 sq2 r2 h2 x1st h2st keep kdec").split()
        s = {n: sem("b_" + n) for n in names}
        s_bw, s_bt, s_cache, s_stl, s_sto = sem("b_weights"), sem("b_tables"), sem("b_cache"), sem("b_state_in"), sem("b_state_out")
        s_copy, s_samp, s_wb, s_fin = sem("b_cache_copy"), sem("b_sample_tables"), sem("b_wb_wo"), sem("b_final_rows")
        s_zero, s_qm, s_kdm, s_sread, s_supd, s_smm = sem("b_zero"), sem("b_qm"), sem("b_kdm"), sem("b_sread"), sem("b_supd"), sem("b_smm")
        s_vstep, s_qbd, s_tab = sem("b_dve_step"), sem("b_qbd"), sem("b_prompt_tables")

        def block_buffers(b_, tag):
            return [sb(b_, n + tag, [P] + shape) for n, shape in (
                ("X", [D]),
                ("Pr", [HA, 2 * P]),
                ("PT", [HA, 2, P]),
                ("qbT", [HB, P]), ("kbT", [HB, P]), ("atm", [HB, P]), ("oaT", [GRP, P]), ("yn", [HB, DV]), ("yT", [KT, P]),
                ("bg", [2 * D]), ("gf", [D]), ("wa", [4, D]), ("sink", [HA]), ("mx", [HA]), ("ngm", [HA]), ("es", [HA]),
                ("rs", [HA]), ("stats", [HB, 6]), ("mv", [HB, 2]), ("sdv", [HB]), ("sm2", [4]))]

        with first as b_:
            X, Pr, PT, qbT, kbT, atm, oaT, yn, yT, bg, gf, wa, sink, mx, ngm, es, rs, stats, mv, sdv, sm2 = block_buffers(b_, "_s")
            sink_s = sb(b_, "sink_col", [P, 1])
            with ExitStack() as keys:
                kcT = sb(keys, "kcT", [P, DEC_B, WINDOW + DEC_S])
            HO = sb(b_, "HO_s", [P, D])
            sb(b_, "keys_rest", [P, DEC_B * (WINDOW + DEC_S) - D])
            vc = sb(b_, "vc", [P, DEC_B, P])
            vn = sb(b_, "vn", [DEC_S, DEC_B, P])
            qbd = sb(b_, "qbd", [P, DEC_B, P])
            alibi_s = sb(b_, "alibi_s", [P, WINDOW + DEC_S])
            intra_s = sb(b_, "intra_s", [P, HB, P])
            into_s = sb(b_, "into_s", [P, HB, P])
            out_s = sb(b_, "out_s", [P, DEC_B, HB])
            st_s = sb(b_, "st_s", [P, HB, DEC_B, DV])
            wb = sb(b_, "wb_s", [P, KT, D])
            with ExitStack() as masked:
                qm = sb(masked, "qm", [P, HB, DEC_B, P])
                kdm = sb(masked, "kdm", [P, DEC_B, HB, DK])
            wo = sb(b_, "wo_s", [P, KT, D])

            mixers, gates = [Z[:, 0:RG]], Z[:, RG:]

            def z(lo, n, half=0):
                return mixers[half][:, lo:lo + n] if lo < RG else gates[:, lo - RG:lo - RG + n]

            def load_mixers(sp, blk, half):
                sp.dma_start(mixers[half], rows(z_d[:, 0:RG], blk)).then_inc(s["z1b" if half else "z1"], 16)

            def wait_mixers(eng, blk, half):
                eng.wait_ge(s["z1b" if half else "z1"], 8 * (blk - half) + 16)

            def load_gates(sp, blk):
                sp.dma_start(gates, rows(z_d[:, RG:], blk)).then_inc(s["z2"], 16)

            def load_rows(sp, blk):
                sp.dma_start(X[:], rows(t["x"], blk)).then_inc(s["xld"], 16)

            def store_block(g, blk):
                g.wait_ge(s["x1"], blk + 1)
                g.sem_inc(s_pool, 1)
                g.dma_start(rows(x1_d, blk), X[:]).then_inc(s["x1st"], 16)
                g.wait_ge(s["h2"], blk + 1)
                g.sem_inc(s_pool, 1)
                g.dma_start(rows(h2_d, blk), HO[:]).then_inc(s["h2st"], 16)

            def pe_transposes(pe, blk, half=0):
                wait_mixers(pe, blk, half)
                for n, lo in enumerate([QA + P * j for j in range(4)] + [QB + P * j for j in range(4)]
                                       + [KB + P * j for j in range(4)] + [KA]):
                    mm = T.transpose(ps[:, n // 4, (n % 4) * P:(n % 4 + 1) * P], z(lo, P, half), ident[:])
                mm.then_inc(s["t1"], 1)

            def pe_gated_transposes(pe, blk):
                pe.wait_ge(s["ysil"], blk + 1)
                for k in range(KT):
                    mm = T.transpose(ps[:, 4 + k // 4, (k % 4) * P:(k % 4 + 1) * P], z(RG + P * k, P), ident[:])
                mm.then_inc(s["yt"], 1)

            def pe_branches(pe, blk):
                pe.wait_ge(s["ytc"], blk + 1)
                pe.wait_ge(s["oatc"], blk + 1)
                for n in range(2):
                    for k in range(4):
                        T.matmul(bank(4 + n), oaT[:, k, :], wa[:, k, n * 512:(n + 1) * 512], start=(k == 0), stop=(k == 3))
                for n in range(2):
                    for k in range(KT):
                        mm = T.matmul(bank(6 + n), yT[:, k, :], wb[:, k, n * 512:(n + 1) * 512], start=(k == 0), stop=(k == KT - 1))
                mm.then_inc(s["ya"], 1)

            def pe_mix_transposes(pe, blk):
                pe.wait_ge(s["mix"], blk + 1)
                for k in range(KT):
                    mm = T.transpose(ps[:, 4 + k // 4, (k % 4) * P:(k % 4 + 1) * P], z(GA + P * k, P), ident[:])
                mm.then_inc(s["mixt"], 1)

            def pe_output(pe, blk):
                pe.wait_ge(s["mixtc"], blk + 1)
                for n in range(2):
                    for k in range(KT):
                        mm = T.matmul(bank(6 + n), yT[:, k, :], wo[:, k, n * 512:(n + 1) * 512], start=(k == 0), stop=(k == KT - 1))
                mm.then_inc(s["wo"], 1)

            def pe_scores_b(pe, blk):
                for h in range(HB):
                    mm = T.matmul(ps[:, 6, h * P:(h + 1) * P], kbT[:, h, :], qbT[:, h, :], start=True, stop=True)
                mm.then_inc(s["st"], 1)

            def act_exps(act, blk, width):
                act.wait_ge(s["sm_d"], blk + 1)
                S.activation(es[:], es[:], ACT.Exp).then_inc(s["es"], 1)
                for h in range(HA):
                    e = S.activation(Pr[:, h, 0:width], Pr[:, h, 0:width], ACT.Exp, bias=ngm[:, h:h + 1], accum_out=rs[:, h:h + 1])
                e.then_inc(s["exp"], 1)

            def act_gate(act, blk):
                act.wait_ge(s["z2"], 16 * blk + 16)
                S.activation(z(RG, D), z(RG, D), ACT.Silu).then_inc(s["silu"], 1)

            def act_sigmoids(act, blk):
                act.wait_ge(s["ga"], blk + 1)
                S.activation(z(GA, 2 * D), z(GA, 2 * D), ACT.Sigmoid).then_inc(s["gates"], 1)

            def act_gated(act, blk):
                act.wait_ge(s["yt"], blk + 1)
                S.activation(yT[:].rearrange("p k n -> p (k n)"), bank(4, 2), ACT.Copy).then_inc(s["ytc"], 1)

            def act_mix(act, blk):
                act.wait_ge(s["mixt"], blk + 1)
                S.activation(yT[:].rearrange("p k n -> p (k n)"), bank(4, 2), ACT.Copy).then_inc(s["mixtc"], 1)

            def act_deviation(act, blk):
                act.wait_ge(s["var"], blk + 1)
                S.activation(sdv[:], sdv[:], ACT.Sqrt).then_inc(s["rs"], 1)

            def act_norm2(act, blk):
                act.wait_ge(s["x1"], blk + 1)
                S.activation(HO[:], X[:], ACT.Square, accum_out=sm2[:, 0:1]).then_inc(s["ssq2"], 1)
                act.wait_ge(s["ms2"], blk + 1)
                S.activation(sm2[:, 2:3], sm2[:, 1:2], ACT.Sqrt).then_inc(s["sq2"], 1)

            def dve_softmax(v, blk, width, sinks, step):
                pr = Pr[:, :, 0:width]
                v.wait_ge(s["sm_s"], blk + 1)
                V.tensor_reduce(mx[:], pr, op=ALU.max, axis=AX.X).then_inc(s["sm_m"], 1)
                v.wait_ge(s["sm_m"], blk + 1)
                V.tensor_tensor(mx[:], mx[:], sinks, ALU.max).then_inc(s["sm_mx"], 1)
                v.wait_ge(s["sm_mx"], blk + 1)
                V.tensor_scalar(ngm[:], mx[:], -1.0, None, ALU.mult).then_inc(s["sm_neg"], 1)
                V.tensor_tensor(es[:], sinks, mx[:], ALU.subtract).then_inc(s["sm_d"], 1)

            def dve_probs(v, blk, width):
                pr = Pr[:, :, 0:width]
                v.wait_ge(s["exp"], blk + 1)
                V.tensor_tensor(rs[:], rs[:], es[:], ALU.add).then_inc(s["den"], 1)
                v.wait_ge(s["den"], blk + 1)
                V.reciprocal(rs[:], rs[:]).then_inc(s["rden"], 1)
                v.wait_ge(s["rden"], blk + 1)
                V.tensor_tensor(pr, pr, rs[:].unsqueeze(2).to_broadcast([P, HA, width]), ALU.mult).then_inc(s["prob"], 1)

            def dve_retention_norm(v, blk, b0, step):
                v.wait_ge(s["ro"], blk + 1)
                for h in range(HB):
                    q = V.bn_stats(stats[:, h, :], ps[:, b0 + h // 2, (h % 2) * DV:(h % 2 + 1) * DV])
                step.did(q)
                step.settle()
                v.sem_inc(s["rok"], 1)
                for h in range(HB):
                    q = V.bn_aggr(mv[:, h, :], stats[:, h, :])
                q.then_inc(s["stats"], 1)
                v.wait_ge(s["stats"], blk + 1)
                V.tensor_scalar(sdv[:], mv[:, :, 1], EPS, None, ALU.add).then_inc(s["var"], 1)
                v.wait_ge(s["rs"], blk + 1)
                V.reciprocal(sdv[:], sdv[:]).then_inc(s["rstd"], 1)
                v.wait_ge(s["rstd"], blk + 1)
                for h in range(HB):
                    q = V.tensor_scalar(yn[:, h, :], ps[:, b0 + h // 2, (h % 2) * DV:(h % 2 + 1) * DV],
                                        mv[:, h, 0:1], sdv[:, h:h + 1], ALU.subtract, ALU.mult)
                q.then_inc(s["yn"], 1)

            def dve_gate(v, blk):
                v.wait_ge(s["yn"], blk + 1)
                v.wait_ge(s["silu"], blk + 1)
                V.tensor_tensor(z(RG, D), z(RG, D), yn[:].rearrange("p h n -> p (h n)"), ALU.mult).then_inc(s["ysil"], 1)
                V.tensor_tensor(z(GA, 2 * D), z(GA, 2 * D), bg[:], ALU.add).then_inc(s["ga"], 1)

            def dve_merge(v, blk):
                v.wait_ge(s["gates"], blk + 1)
                v.wait_ge(s["ya"], blk + 1)
                V.tensor_tensor(z(GA, D), z(GA, D), bank(4, 2), ALU.mult).then_inc(s["mixa"], 1)
                V.tensor_tensor(z(GB, D), z(GB, D), bank(6, 2), ALU.mult).then_inc(s["mixb"], 1)
                v.wait_ge(s["mixb"], blk + 1)
                V.tensor_tensor(z(GA, D), z(GA, D), z(GB, D), ALU.add).then_inc(s["mix"], 1)

            def dve_residual(v, blk):
                v.wait_ge(s["wo"], blk + 1)
                v.wait_ge(s["xld"], 16 * blk + 16)
                V.tensor_tensor(X[:], X[:], bank(6, 2), ALU.add).then_inc(s["x1"], 1)

            def dve_norm2(v, blk):
                v.wait_ge(s["ssq2"], blk + 1)
                V.tensor_scalar(sm2[:, 1:2], sm2[:, 0:1], 1.0 / D, EPS, ALU.mult, ALU.add).then_inc(s["ms2"], 1)
                v.wait_ge(s["sq2"], blk + 1)
                V.reciprocal(sm2[:, 3:4], sm2[:, 2:3]).then_inc(s["r2"], 1)
                v.wait_ge(s["r2"], blk + 1)
                V.scalar_tensor_tensor(HO[:], X[:], sm2[:, 3:4], gf[:], ALU.mult, ALU.mult).then_inc(s["h2"], 1)

            with nc.Block() as block:
                @block.sync
                def _(sp):
                    sp.sem_inc(s["z1"], 16)
                    sp.sem_inc(s["z2"], 16)
                    sp.dma_start(z_d[0:P, KA:QB], z(KA, QB - KA)).then_inc(s_kv, 16)
                    sp.dma_start(kcT[:, :, 0:WINDOW], t["cache_kt"].rearrange("p (b w) -> p b w", b=DEC_B)).then_inc(s_cache, 16)
                    sp.dma_start(vc[:], t["cache_v"].rearrange("(b w) c -> w b c", w=WINDOW)).then_inc(s_cache, 16)
                    sp.dma_start(into_s[:].rearrange("p h n -> p (h n)"), t["into_s"]).then_inc(s_samp, 16)
                    sp.dma_start(out_s[:].rearrange("p h n -> p (h n)"), t["out_dec_s"]).then_inc(s_samp, 16)
                    sp.dma_start(alibi_s[:], t["alibi_s"]).then_inc(s_samp, 16)
                    sp.dma_start(intra_s[:].rearrange("p h n -> p (h n)"), t["intra_s"]).then_inc(s_samp, 16)
                    sp.dma_start(sink_s[:], t["sinks_rows"]).then_inc(s_bw, 16)
                    for h in range(HB):
                        sp.dma_start(st_s[:, h], t["state"].rearrange("(b h p) v -> h p b v", h=HB, p=DK)[h]).then_inc(s_stl, 16)
                    sp.wait_ge(s_kv, 16)
                    sp.dma_start(vn[:], z_d[0:P, VA:VA + P].rearrange("(b n) c -> n b c", n=DEC_S)).then_inc(s_cache, 16)
                    sp.dma_start(bg[:], t["b_gate"].to_broadcast([P, 2 * D])).then_inc(s_bw, 16)
                    sp.dma_start(gf[:], t["norm_ffn"].to_broadcast([P, D])).then_inc(s_bw, 16)
                    sp.dma_start(wa[:], t["w_branch_a"].rearrange("(k p) n -> p k n", p=P)).then_inc(s_bw, 16)
                    sp.dma_start(wb[:], t["w_branch_b"].rearrange("(k p) n -> p k n", p=P)).then_inc(s_wb, 16)
                    for src, dst, lo in ((t["cache_k"], o["kc"], KA), (t["cache_v"], o["vc"], VA)):
                        r = dst.rearrange("(b w) c -> b w c", w=WINDOW)
                        sp.dma_start(r[:, 0:WINDOW - DEC_S], src.rearrange("(b w) c -> b w c", w=WINDOW)[:, DEC_S:]).then_inc(s_copy, 16)
                        sp.dma_start(r[:, WINDOW - DEC_S:], z_d[0:P, lo:lo + P].rearrange("(b n) c -> b n c", n=DEC_S)).then_inc(s_copy, 16)
                    sp.wait_ge(s["ro"], 1)
                    sp.wait_ge(s_smm, HB)
                    sp.dma_start(wo[:], t["w_out"].rearrange("(k p) n -> p k n", p=P)).then_inc(s_wb, 16)
                    for h in range(HB):
                        sp.wait_ge(s_supd, h + 1)
                        sp.dma_start(o["ss"].rearrange("(b h p) v -> h p b v", h=HB, p=DK)[h], st_s[:, h]).then_inc(s_sto, 16)
                    sp.wait_ge(s_sto, 16 * HB)
                    sp.wait_ge(s_copy, 16 * 4)

                @block.gpsimd
                def _(g):
                    load_rows(g, 0)
                    store_block(g, 0)
                    g.wait_ge(s["x1st"], 16)
                    g.wait_ge(s["h2st"], 16)

                @block.tensor
                def _(pe):
                    pe.wait_ge(s_const, 16)
                    pe_transposes(pe, 0)
                    pe.wait_ge(s_qbd, 1)
                    pe.wait_ge(s["qkv"], 2)
                    for b in range(DEC_B):
                        mm = T.matmul(ps[:, 4 + b // 2, (b % 2) * 144:(b % 2) * 144 + 144], qbd[:, b, :], kcT[:, b, :], start=True, stop=True)
                    mm.then_inc(s["scores"], 1)
                    pe.wait_ge(s["prob"], 1)
                    for b in range(DEC_B):
                        T.transpose(ps[:, b // 4, (b % 4) * P:(b % 4 + 1) * P], Pr[:, b, 0:P], ident[:])
                    for b in range(DEC_B):
                        mm = T.transpose(ps[0:DEC_S, 2 + b // 4, (b % 4) * P:(b % 4 + 1) * P], Pr[:, b, P:P + DEC_S], ident[:])
                    mm.then_inc(s["pt"], 1)
                    pe.wait_ge(s["ptc"], 2)
                    for b in range(DEC_B):
                        for kv in range(KV):
                            d = ps[HD * kv:HD * kv + HD, 4, :].rearrange("p (j t) -> p j t", j=GRP)[:, :, b * DEC_S:(b + 1) * DEC_S]
                            T.matmul(d, vc[:, b, HD * kv:HD * kv + HD], PT[:, b, 0, HD * kv:HD * kv + HD], start=True, stop=False)
                            mm = T.matmul(d, vn[:, b, HD * kv:HD * kv + HD], PT[0:DEC_S, b, 1, HD * kv:HD * kv + HD], start=False, stop=True)
                    mm.then_inc(s["oat"], 1)
                    pe.wait_ge(s["sm_s"], 1)
                    pe_scores_b(pe, 0)
                    pe.wait_ge(s["atm"], 1)
                    pe.wait_ge(s_qm, 1)
                    pe.wait_ge(s_stl, 16 * HB)
                    for h in range(HB):
                        d = ps[:, 6 + h // 2, (h % 2) * DV:(h % 2 + 1) * DV]
                        mm = T.matmul(d, atm[:, h, :], z(VB + h * DV, DV), start=True, stop=False)
                        for b in range(DEC_B):
                            mm = T.matmul(d, qm[:, h, b, :], st_s[:, h, b, :], start=False, stop=(b == DEC_B - 1))
                    mm.then_inc(s["ro"], 1)
                    pe.wait_ge(s_kdm, 1)
                    for h in range(HB):
                        if h == 1:
                            pe_gated_transposes(pe, 0)
                            pe.wait_ge(s_bw, 16 * 4)
                            pe.wait_ge(s_wb, 16)
                            pe_branches(pe, 0)
                        if h:
                            pe.wait_ge(s_supd, h)
                        for b in range(DEC_B):
                            mm = T.matmul(ps[:, b // 2, (b % 2) * DV:(b % 2 + 1) * DV], kdm[:, b, h, :], z(VB + h * DV, DV), start=True, stop=True)
                        mm.then_inc(s_smm, 1)
                    pe_mix_transposes(pe, 0)
                    pe.wait_ge(s_wb, 32)
                    pe_output(pe, 0)

                @block.scalar
                def _(act):
                    act_gate(act, 0)
                    act.wait_ge(s["t1"], 1)
                    act.wait_ge(s_cache, 48)
                    S.activation(kcT[:, :, WINDOW:], ps[:, 3, 0:P].rearrange("p (b n) -> p b n", b=DEC_B), ACT.Copy).then_inc(s["qkv"], 1)
                    S.activation(kbT[:].rearrange("p h n -> p (h n)"), bank(2), ACT.Copy).then_inc(s["qkv"], 1)
                    act_exps(act, 0, WINDOW + DEC_S)
                    act.wait_ge(s["pt"], 1)
                    S.activation(PT[:, :, 0, :], bank(0, 2).rearrange("p (b n) -> p b n", b=DEC_B), ACT.Copy).then_inc(s["ptc"], 1)
                    act_deviation(act, 0)
                    act_gated(act, 0)
                    act_sigmoids(act, 0)
                    act_mix(act, 0)
                    act_norm2(act, 0)

                @block.vector
                def _(v):
                    V.memset(qbd[:], 0.0).then_inc(s_zero, 1)
                    V.memset(qm[:], 0.0).then_inc(s_zero, 1)
                    v.wait_ge(s_zero, 2)
                    v.wait_ge(s["t1"], 1)
                    for kv in range(KV):
                        q = V.tensor_copy(qbd[HD * kv:HD * kv + HD, :, HD * kv:HD * kv + HD].rearrange("p b (j n) -> p j b n", j=GRP),
                                          ps[HD * kv:HD * kv + HD, 0, :].rearrange("p (j b n) -> p j b n", j=GRP, b=DEC_B))
                    V.tensor_copy(qbT[:].rearrange("p h n -> p (h n)"), bank(1)).then_inc(s_qbd, 1)
                    v.wait_ge(s_samp, 64)
                    diag = bass.AP(tensor=qm[:].tensor, offset=qm[:].offset,
                                   ap=[list(qm[:].ap[0]), [DEC_B * P, HB], [P + DEC_S, DEC_B], [1, DEC_S]])
                    V.tensor_tensor(diag, bank(1).rearrange("p (h b n) -> p h b n", h=HB, b=DEC_B),
                                    into_s[:].rearrange("p h (b n) -> p h b n", b=DEC_B), ALU.mult).then_inc(s_qm, 1)
                    v.wait_ge(s["z1"], 16)
                    for b in range(DEC_B):
                        q = V.tensor_tensor(kdm[:, b], z(KB, HB * DK).rearrange("p (h d) -> p h d", h=HB),
                                            out_s[:, b, :].unsqueeze(2).to_broadcast([P, HB, DK]), ALU.mult)
                    q.then_inc(s_kdm, 1)
                    v.wait_ge(s["scores"], 1)
                    v.wait_ge(s_bw, 64)
                    for b in range(DEC_B):
                        q = V.scalar_tensor_tensor(Pr[:, b, 0:144], ps[:, 4 + b // 2, (b % 2) * 144:(b % 2) * 144 + 144],
                                                   HD ** -0.5, alibi_s[:], ALU.mult, ALU.add)
                    q.then_inc(s["sm_s"], 1)
                    dve_softmax(v, 0, 144, sink_s[:].to_broadcast([P, DEC_B]), None)
                    dve_probs(v, 0, 144)
                    v.wait_ge(s["pt"], 1)
                    V.tensor_copy(PT[0:DEC_S, :, 1, :], ps[0:DEC_S, 2:4, :].rearrange("p c (b n) -> p (c b) n", n=P)).then_inc(s["ptc"], 1)
                    v.wait_ge(s["oat"], 1)
                    V.tensor_copy(oaT[:].rearrange("p j n -> p (j n)"), bank(4)).then_inc(s["oatc"], 1)
                    v.wait_ge(s["st"], 1)
                    V.tensor_tensor(atm[:].rearrange("p h n -> p (h n)"), bank(6), intra_s[:].rearrange("p h n -> p (h n)"), ALU.mult).then_inc(s["atm"], 1)
                    dve_retention_norm(v, 0, 6, Steps(v, s_vstep))
                    dve_gate(v, 0)
                    for h in range(HB):
                        v.wait_ge(s_smm, h + 1)
                        V.scalar_tensor_tensor(st_s[:, h].rearrange("p b n -> p (b n)"), st_s[:, h].rearrange("p b n -> p (b n)"),
                                               math.exp(DEC_S * LOG_DECAY[h]), bank(0, 4), ALU.mult, ALU.add).then_inc(s_supd, 1)
                    dve_merge(v, 0)
                    dve_residual(v, 0)
                    dve_norm2(v, 0)

        c = {n: sem("c_" + n) for n in "hld ht hcp htc q qc qt qtc sc scc v1 cand b2 ab abf idxf idx gd ge gsum gr gate".split()}
        d = {n: sem("d_" + n) for n in "x1 nf freed gelu act wgt accz y ssq ms sq r yo yst ixl ixd pool gtc".split()}
        s_cw, s_cgate = sem("c_weights"), sem("c_carry")
        s_ring = [sem(f"d_ring{i}") for i in range(RING)]
        UG = NK // PH
        ORDER = [("u", 0)] + [x for g in range(1, PH) for x in (("u", g), ("v", g - 1))] + [("v", PH - 1)]
        USES = 2 * NK // RING
        def search_buffers(stack, tag):
            return [sb(stack, n + tag, [P] + shape, dt) for n, shape, dt in (
                ("kt", [2, NKEY], f32), ("io", [TOPK], f32), ("H", [D], f32), ("hT", [KT, P], f32), ("SC", [16, NKEY], f32),
                ("VV", [16, TOPK], f32), ("II", [16, TOPK], u32), ("IF", [16, TOPK], f32), ("CA", [PH, TOPK * TOPK], f32),
                ("BV", [PH, TOPK], f32), ("BP", [PH, TOPK], u32), ("AU", [2, NK], u32), ("AF", [2, NK], f32),
                ("I12", [2, NK], f32), ("IX", [NK], u32), ("GT", [PH, TOPK], f32), ("GS", [PH], f32), ("IXD", [NK], u32),
                ("GD", [NK], f32), ("DOT", [NK], f32), ("GE", [NK], f32), ("WG", [NK], f32), ("nf", [D], f32), ("m4", [4], f32))]

        def load_search(sp):
            sp.dma_start(kt[:, 0], t["sub_k1t"]).then_inc(s_cw, 16)
            sp.dma_start(kt[:, 1], t["sub_k2t"]).then_inc(s_cw, 16)
            sp.dma_start(io[:], t["iota16"]).then_inc(s_cw, 16)
            for k in range(KT):
                sp.dma_start(wq[:, k], t["peer_w_q"][k * P:(k + 1) * P, :]).then_inc(s_cw, 16)

        def pe_keys(pe, blk):
            pe.wait_ge(c["hld"], 16 * blk + 16)
            pe.wait_ge(c["v1"], blk + 1)
            for k in range(KT):
                mm = T.transpose(ps[:, k // 4, (k % 4) * P:(k % 4 + 1) * P], H[:, k * P:(k + 1) * P], ident[:])
            mm.then_inc(c["ht"], 1)
            pe.wait_ge(c["htc"], blk + 1)
            for n in range(4):
                for k in range(KT):
                    mm = T.matmul(bank(4 + n), hT[:, k, :], wq[:, k, n * 512:(n + 1) * 512], start=(k == 0), stop=(k == KT - 1))
                mm.then_inc(c["q"], 1)
            pe.wait_ge(c["qc"], 2 * blk + 2)
            for n in range(16):
                mm = T.transpose(ps[:, n // 4, (n % 4) * P:(n % 4 + 1) * P], Q[:, n, :], ident[:])
            mm.then_inc(c["qt"], 1)
            pe.wait_ge(c["qtc"], 2 * blk + 2)
            for n in range(16):
                mm = T.matmul(ps[:, 4 + n // 4, (n % 4) * P:(n % 4 + 1) * P], qT[:, n, :], kt[:, n % 2, :], start=True, stop=True)
            mm.then_inc(c["sc"], 1)

        def act_keys_first(act, blk):
            act.wait_ge(c["ht"], blk + 1)
            S.activation(hT[:].rearrange("p k n -> p (k n)"), bank(0, 2), ACT.Copy).then_inc(c["htc"], 1)
            act.wait_ge(c["q"], 4 * blk + 2)
            S.activation(Q[:, 0:8].rearrange("p k n -> p (k n)"), bank(4, 2), ACT.Copy).then_inc(c["qc"], 1)

        def act_keys_second(act, blk):
            act.wait_ge(c["q"], 4 * blk + 4)
            S.activation(Q[:, 8:16].rearrange("p k n -> p (k n)"), bank(6, 2), ACT.Copy).then_inc(c["qc"], 1)
            act.wait_ge(c["qt"], blk + 1)
            for i in range(2):
                S.activation(qT[:, 8 * i:8 * i + 8].rearrange("p k n -> p (k n)"), bank(2 * i, 2), ACT.Copy).then_inc(c["qtc"], 1)
            act.wait_ge(c["sc"], blk + 1)
            act.wait_ge(c["scc"], blk + 1)
            S.activation(SC[:].rearrange("p k n -> p (k n)"), bank(4, 4), ACT.Copy).then_inc(c["v1"], 1)

        def act_gates(act, blk):
            act.wait_ge(c["gd"], blk + 1)
            S.activation(GT[:], GT[:], ACT.Exp).then_inc(c["ge"], 1)

        def act_gelu(act, blk, grp):
            act.wait_ge(d["act"], PH * blk + grp + 1)
            cols = slice(grp * UG, (grp + 1) * UG)
            S.activation(GE[:, cols], DOT[:, cols], ACT.Gelu_apprx_tanh).then_inc(d["gelu"], 1)

        def act_norm(act, blk):
            act.wait_ge(d["y"], blk + 1)
            S.activation(ACC[:, 1], ACC[:, 0], ACT.Square, accum_out=m4[:, 0:1]).then_inc(d["ssq"], 1)
            act.wait_ge(d["ms"], blk + 1)
            S.activation(m4[:, 2:3], m4[:, 1:2], ACT.Sqrt).then_inc(d["sq"], 1)

        def pool_gathers(g, blk):
            g.wait_ge(d["ixd"], blk + 1)
            g.sem_inc(d["pool"], 1)
            for n in range(2 * NK):
                kind, grp = ORDER[n // UG]
                if n % 4 == 0:
                    g.wait_ge(d["freed"], 2 * NK * blk + n + 4)
                    g.sem_inc(d["pool"], 1)
                if (kind, n % UG) == ("u", 0) and grp == PH - 1:
                    g.wait_ge(d["ixl"], blk + 1)
                    g.sem_inc(d["pool"], 1)
                k = grp * UG + n % UG
                gather = g.indirect_dma_start(ring[:, n % RING, :], None, t["peer_u"] if kind == "u" else t["peer_v"],
                                              bass.IndirectOffsetOnAxis(ap=IXD[:, k:k + 1], axis=0))
                gather.then_inc(s_ring[n % RING], 16)

        def carry(v):
            v.sem_inc(s_cgate, 1)

        def dve_maxima(vals, src, lo, n, step):
            for i in range(n):
                q = V.max(vals[:, i, lo:lo + 8], src[:, i, :])
            step.did(q)

        def dve_places(pos, vals, src, lo, n):
            for i in range(n):
                q = V.max_index(pos[:, i, lo:lo + 8], vals[:, i, lo:lo + 8], src[:, i, :])
            return q

        def dve_replace(vals, src, n, step):
            for i in range(n):
                q = V.match_replace(src[:, i, :], vals[:, i, 0:8], src[:, i, :], LOW)
            step.did(q)

        PARTS = 20

        def dve_keys(part, v, blk, step):
            if part == 0:
                v.wait_ge(c["v1"], blk + 2)
            elif part in (6, 11):
                v.wait_ge(c["cand"] if part == 6 else c["b2"], blk + 1)
            elif part == 5:
                v.wait_ge(c["scc"], blk + 2)
            elif part == 12:
                v.wait_ge(c["abf"], blk + 1)
            elif part != 19:
                step.settle()
            if part < 11:
                carry(v)
            oh = CA[:].rearrange("p h (k i) -> p (h k) i", i=TOPK)
            oh4 = CA[:].rearrange("p h (k i) -> p h k i", i=TOPK)
            if part in (0, 3):
                dve_maxima(VV, SC, 0 if part == 0 else 8, 16, step)
            elif part == 1:
                step.did(dve_places(II, VV, SC, 0, 16))
            elif part == 2:
                dve_replace(VV, SC, 16, step)
            elif part == 4:
                dve_places(II, VV, SC, 8, 16).then_inc(c["scc"], 1)
            elif part == 5:
                step.did(V.tensor_copy(IF[:], II[:]))
                V.tensor_tensor(CA[:].rearrange("p h (i j) -> p h i j", i=TOPK),
                                VV[:, 0::2, :].unsqueeze(3).to_broadcast([P, PH, TOPK, TOPK]),
                                VV[:, 1::2, :].unsqueeze(2).to_broadcast([P, PH, TOPK, TOPK]), ALU.add).then_inc(c["cand"], 1)
            elif part in (6, 9):
                dve_maxima(BV, CA, 0 if part == 6 else 8, PH, step)
            elif part == 7:
                step.did(dve_places(BP, BV, CA, 0, PH))
            elif part == 8:
                dve_replace(BV, CA, PH, step)
            elif part == 10:
                dve_places(BP, BV, CA, 8, PH).then_inc(c["b2"], 1)
            elif part == 11:
                v.wait_ge(d["gtc"], blk + 1)
                V.tensor_tensor(GT[:], BV[:], BV[:, :, 0:1].to_broadcast([P, PH, TOPK]), ALU.subtract).then_inc(c["gd"], 1)
                bp = BP[:].rearrange("p h k -> p (h k)")
                V.tensor_scalar(AU[:, 0], bp, 4, None, ALU.logical_shift_right)
                V.tensor_scalar(AU[:, 1], bp, 15, None, ALU.bitwise_and).then_inc(c["ab"], 1)
                v.wait_ge(c["ab"], blk + 1)
                V.tensor_copy(AF[:], AU[:]).then_inc(c["abf"], 1)
            elif part in (12, 15):
                step.did(V.tensor_tensor(oh, AF[:, (part - 12) // 3, :].unsqueeze(2).to_broadcast([P, NK, TOPK]),
                                         io[:].unsqueeze(1).to_broadcast([P, NK, TOPK]), ALU.is_equal))
            elif part in (13, 16):
                step.did(V.tensor_tensor(oh4, oh4, IF[:, (part - 13) // 3::2, :].unsqueeze(2).to_broadcast([P, PH, TOPK, TOPK]), ALU.mult))
            elif part in (14, 17):
                step.did(V.tensor_reduce(I12[:, (part - 14) // 3, :], oh, op=ALU.add, axis=AX.X))
            elif part == 18:
                V.scalar_tensor_tensor(I12[:, 0, :], I12[:, 0, :], float(NKEY), I12[:, 1, :], ALU.mult, ALU.add).then_inc(c["idxf"], 1)
                v.wait_ge(c["idxf"], blk + 1)
                V.tensor_copy(IX[:], I12[:, 0, :]).then_inc(c["idx"], 1)
            elif part == 19:
                v.wait_ge(c["ge"], blk + 1)
                V.tensor_reduce(GS[:], GT[:], op=ALU.add, axis=AX.X).then_inc(c["gsum"], 1)
                v.wait_ge(c["gsum"], blk + 1)
                V.reciprocal(GS[:], GS[:]).then_inc(c["gr"], 1)
                v.wait_ge(c["gr"], blk + 1)
                V.tensor_tensor(GT[:], GT[:], GS[:].unsqueeze(2).to_broadcast([P, PH, TOPK]), ALU.mult).then_inc(c["gate"], 1)

        def dve_hand_over(v, blk):
            v.wait_ge(c["hld"], 16 * blk + 16)
            V.tensor_copy(H2[:], H[:]).then_inc(c["hcp"], 1)
            v.wait_ge(c["gate"], blk + 1)
            V.tensor_copy(GD[:], GT[:].rearrange("p h k -> p (h k)")).then_inc(d["gtc"], 1)

        def dve_hand_over_places(v, blk):
            v.wait_ge(c["idx"], blk + 1)
            V.tensor_copy(IXD[:, 0:NK - UG], IX[:, 0:NK - UG]).then_inc(d["ixd"], 1)

        def dve_hand_over_last_places(v):
            V.tensor_copy(IXD[:, NK - UG:], IX[:, NK - UG:]).then_inc(d["ixl"], 1)

        FIRST_PART = 7

        def dve_experts(v, blk, more):
            if more:
                step = Steps(v, s_vstep, STEPS_C + DVE_C * (blk + 1))
            v.wait_ge(c["hcp"], blk + 1)
            v.wait_ge(d["gtc"], blk + 2)
            for n in range(2 * NK):
                kind, grp = ORDER[n // UG]
                k = grp * UG + n % UG
                if more and n % (UG // 2) == 0:
                    part = n // (UG // 2) - FIRST_PART
                    if 0 <= part < PARTS:
                        dve_keys(part, v, blk + 1, step)
                if kind == "v" and n % UG == 0:
                    cols = slice(grp * UG, (grp + 1) * UG)
                    v.wait_ge(d["gelu"], PH * blk + grp + 1)
                    V.tensor_tensor(WG[:, cols], GE[:, cols], GD[:, cols], ALU.mult).then_inc(d["wgt"], 1)
                    v.wait_ge(d["wgt"], PH * blk + grp + 1)
                    if more and grp == PH - 1:
                        dve_hand_over(v, blk + 1)
                if more and n == 2 * NK - UG // 2:
                    dve_hand_over_places(v, blk + 1)
                row = ring[:, n % RING, :]
                v.wait_ge(s_ring[n % RING], USES * 16 * blk + 16 * (n // RING + 1))
                if kind == "u":
                    V.tensor_tensor_reduce(out=row, in0=row, in1=H2[:], scale=1.0, scalar=0.0, op0=ALU.mult,
                                           op1=ALU.add, accum_out=DOT[:, k:k + 1]).then_inc(d["freed"], 1)
                    if n % UG == UG - 1:
                        v.wait_ge(d["freed"], 2 * NK * blk + RING + n + 1)
                        v.sem_inc(d["act"], 1)
                elif k < 2:
                    V.tensor_scalar(ACC[:, k], row, WG[:, k:k + 1], None, ALU.mult).then_inc(d["freed"], 1)
                else:
                    v.wait_ge(d["freed"], 2 * NK * blk + RING + n - 1)
                    V.scalar_tensor_tensor(ACC[:, k % 2], row, WG[:, k:k + 1], ACC[:, k % 2], ALU.mult, ALU.add).then_inc(d["freed"], 1)
            if more:
                dve_hand_over_last_places(v)
            v.wait_ge(d["freed"], 2 * NK * blk + RING + 2 * NK)
            V.tensor_tensor(ACC[:, 0], ACC[:, 0], ACC[:, 1], ALU.add).then_inc(d["accz"], 1)
            v.wait_ge(d["accz"], blk + 1)
            v.wait_ge(d["x1"], 16 * blk + 16)
            V.tensor_tensor(ACC[:, 0], ACC[:, 0], X1[:], ALU.add).then_inc(d["y"], 1)
            v.wait_ge(d["ssq"], blk + 1)
            V.tensor_scalar(m4[:, 1:2], m4[:, 0:1], 1.0 / D, EPS, ALU.mult, ALU.add).then_inc(d["ms"], 1)
            v.wait_ge(d["sq"], blk + 1)
            V.reciprocal(m4[:, 3:4], m4[:, 2:3]).then_inc(d["r"], 1)
            v.wait_ge(d["r"], blk + 1)
            V.scalar_tensor_tensor(X1[:], ACC[:, 0], m4[:, 3:4], nf[:], ALU.mult, ALU.mult).then_inc(d["yo"], 1)

        with ExitStack() as m:
            kt, io, H, hT, SC, VV, II, IF, CA, BV, BP, AU, AF, I12, IX, GT, GS, IXD, GD, DOT, GE, WG, nf, m4 = search_buffers(m, "_s")
            with ExitStack() as q_:
                wq = sb(q_, "wq_s", [P, KT, PH * 256])
                Q = sb(q_, "Q_s", [P, 16, P])
                qT = sb(q_, "qT_s", [P, 16, P])
            ring = sb(m, "ring_s", [P, RING, D])
            ACC = sb(m, "ACC_s", [P, 2, D])
            X1 = sb(m, "X1_s", [P, D])
            H2 = sb(m, "H2_s", [P, D])
            PB = NB - 1
            xg = sb(m, "xg", [P, KT, PB * P])
            w = sb(m, "w", [P, 2, KT, WC])
            zo = sb(m, "zo", [P, 2, PB, WC])
            z_t = z_d[P:, :].rearrange("(b p) c -> p b c", p=P)
            GATES_AT, GELU_AT = 16, [24 + 11 * g for g in range(PH)]

            with nc.Block() as block:
                @block.sync
                def _(sp):
                    sp.dma_start(H[:], rows(h2_d, 0)).then_inc(c["hld"], 16)
                    load_search(sp)
                    for k in range(KT):
                        sp.dma_start(xg[:, k, :], t["x_t"][k * P:(k + 1) * P, P:]).then_inc(s_xt, 16)
                    for p in range(2):
                        sp.dma_start(w[:, p].rearrange("p k c -> p (k c)"), t["w_in"][p * P:(p + 1) * P, :]).then_inc(s_w[p], 16)
                    sp.dma_start(nf[:], t["norm_final"].to_broadcast([P, D])).then_inc(d["nf"], 16)
                    for lo, hi in ((1, 4), (4, WT // 2)):
                        with sp.Fori(lo, hi) as i:
                            for p in range(2):
                                sp.wait_ge(s_mm, WT + PB * (2 * i + p - 1))
                                sp.dma_start(w[:, p].rearrange("p k c -> p (k c)"),
                                             t["w_in"][bass.ds((2 * i + p) * P, P), :]).then_inc(s_w[p], 16)
                        if lo == 1:
                            sp.wait_ge(c["sc"], 1)
                            sp.dma_start(X1[:], rows(x1_d, 0)).then_inc(d["x1"], 16)
                    sp.wait_ge(d["yo"], 1)
                    sp.dma_start(rows(o["y"], 0), X1[:]).then_inc(d["yst"], 16)
                    sp.wait_ge(d["yst"], 16)

                @block.tensor
                def _(pe):
                    pe.wait_ge(s_cw, 16 * (KT + 3))
                    pe_keys(pe, 0)
                    pe.wait_ge(c["v1"], 2)
                    pe.wait_ge(s_xg, 2 * KT)
                    with pe.Fori(0, WT // 2) as i:
                        for n in range(2 * PB):
                            p, b = n // PB, n % PB
                            if b == 0:
                                pe.wait_ge(s_w[p], 16 * (WT // 4) + 16 * i + 16)
                            pe.wait_ge(s_zact, WT + 2 * PB * i + n + 1)
                            for k in range(KT):
                                mm = T.matmul(ps[:, n % AB, 0:WC], xg[:, k, b * P:(b + 1) * P], w[:, p, k, :],
                                              start=(k == 0), stop=(k == KT - 1))
                            mm.then_inc(s_mm, 1)

                @block.scalar
                def _(act):
                    act.sem_inc(c["v1"], 1)
                    act.sem_inc(s_zact, AB)
                    act_keys_first(act, 0)
                    act_keys_second(act, 0)
                    for n in range(WT * PB):
                        if n == GATES_AT:
                            act_gates(act, 0)
                        if n in GELU_AT:
                            act_gelu(act, 0, GELU_AT.index(n))
                        tile, b = n // PB, n % PB
                        if b == 0 and tile >= 2:
                            act.wait_ge(s_zst[tile % 2], 16 * (tile // 2))
                        act.wait_ge(s_mm, WT + n + 1)
                        S.activation(zo[:, tile % 2, b, :], ps[:, n % AB, 0:WC], ACT.Copy, scale=rstd[:, b + 1:b + 2]).then_inc(s_zact, 1)
                        if b == PB - 1:
                            act.wait_ge(s_zact, WT + AB + n + 1)
                            act.dma_start(z_t[:, :, tile * WC:(tile + 1) * WC], zo[:, tile % 2]).then_inc(s_zst[tile % 2], 16)
                    act_norm(act, 0)
                    for p in range(2):
                        act.wait_ge(s_zst[p], 16 * (WT // 2))

                @block.vector
                def _(v):
                    v.sem_inc(c["scc"], 1)
                    v.sem_inc(d["gtc"], 1)
                    v.sem_inc(d["freed"], RING)
                    v.wait_ge(s_xt, 16 + 16 * KT)
                    for k in range(KT):
                        V.tensor_scalar(xg[:, k, :], xg[:, k, :], gm[:, k:k + 1], None, ALU.mult).then_inc(s_xg, 1)
                    v.wait_ge(s_cw, 16 * (KT + 3))
                    v.wait_ge(d["nf"], 16)
                    step = Steps(v, s_vstep, 1)
                    for part in range(PARTS):
                        dve_keys(part, v, 0, step)
                    assert step.n == DVE_C, step.n
                    dve_hand_over(v, 0)
                    dve_hand_over_places(v, 0)
                    dve_hand_over_last_places(v)
                    dve_experts(v, 0, False)

                @block.gpsimd
                def _(g):
                    pool_gathers(g, 0)


        with ExitStack() as b_:
            mixers = [sb(b_, f"mixers{i}", [P, RG])[:] for i in range(2)]
            gates = sb(b_, "gates", [P, D_IN - RG])[:]
            X, Pr, PT, qbT, kbT, atm, oaT, yn, yT, bg, gf, wa, sink, mx, ngm, es, rs, stats, mv, sdv, sm2 = block_buffers(b_, "_p")
            HO = sb(b_, "HO", [P, D])
            qaT = sb(b_, "qaT", [P, GRP, P])
            kaT = sb(b_, "kaT", [P, 2, P])
            va = sb(b_, "va", [P, 2, P])
            qdT = sb(b_, "qdT", [P, HB, P])
            alibi = sb(b_, "alibi", [P, HA, 2 * P])
            alibi_c = sb(b_, "alibi_c", [P, HA, P])
            intra = sb(b_, "intra", [P, HB, P])
            into = sb(b_, "into", [P, HB, P])
            outd = sb(b_, "outd", [P, HB])
            kdec = sb(b_, "kdec", [P, HB, DK])
            st = sb(b_, "st", [P, HB, DV])
            wb = sb(b_, "wb", [P, KT, D])
            wo = sb(b_, "wo", [P, KT, D])

            def pe_block(pe, blk, half, merge):
                pe_transposes(pe, blk, half)
                if merge:
                    pe_gated_transposes(pe, blk - 1)
                pe.wait_ge(s["qkv"], 2 * blk + 2)
                for kv in range(KV):
                    for j in range(GRP):
                        mm = T.matmul(ps[:, 2 * kv + j // 2, (j % 2) * 256:(j % 2 + 1) * 256], qaT[HD * kv:HD * kv + HD, j, :],
                                      kaT[HD * kv:HD * kv + HD, :, :].rearrange("p s n -> p (s n)"), start=True, stop=True)
                mm.then_inc(s["scores"], 1)
                pe_scores_b(pe, blk)
                pe.wait_ge(s["atm"], blk + 1)
                if merge:
                    pe_branches(pe, blk - 1)
                pe.wait_ge(s["prob"], blk + 1)
                for n in range(2 * HA):
                    mm = T.transpose(ps[:, n // 4, (n % 4) * P:(n % 4 + 1) * P], Pr[:, n // 2, (n % 2) * P:(n % 2 + 1) * P], ident[:])
                mm.then_inc(s["pt"], 1)
                if merge:
                    pe_mix_transposes(pe, blk - 1)
                pe.wait_ge(s["ptc"], 2 * blk + 2)
                for kv in range(KV):
                    for j in range(GRP):
                        for c in range(2):
                            mm = T.matmul(ps[HD * kv:HD * kv + HD, 0, j * P:(j + 1) * P], va[:, c, HD * kv:HD * kv + HD],
                                          PT[:, GRP * kv + j, c, :], start=(c == 0), stop=(c == 1))
                mm.then_inc(s["oat"], 1)
                pe.wait_ge(s["stn"], blk)
                for h in range(HB):
                    d = ps[:, 2 + h // 2, (h % 2) * DV:(h % 2 + 1) * DV]
                    T.matmul(d, atm[:, h, :], z(VB + h * DV, DV, half), start=True, stop=False)
                    mm = T.matmul(d, qdT[:, h, :], st[:, h, :], start=False, stop=True)
                mm.then_inc(s["ro"], 1)
                if merge:
                    pe_output(pe, blk - 1)
                for h in range(HB):
                    mm = T.matmul(ps[:, 4 + h // 2, (h % 2) * DV:(h % 2 + 1) * DV], kdec[:, h, :], z(VB + h * DV, DV, half), start=True, stop=True)
                mm.then_inc(s["kvp"], 1)
                pe.wait_ge(s["yn"], blk + 1)

            def act_block(act, blk, half, merge):
                if merge:
                    act_gate(act, blk - 1)
                act.wait_ge(s["t1"], blk + 1)
                S.activation(qaT[:].rearrange("p h n -> p (h n)"), bank(0), ACT.Copy)
                S.activation(kbT[:].rearrange("p h n -> p (h n)"), bank(2), ACT.Copy).then_inc(s["qkv"], 1)
                if merge:
                    act_gated(act, blk - 1)
                act_exps(act, blk, 2 * P)
                if merge:
                    act_sigmoids(act, blk - 1)
                act.wait_ge(s["pt"], blk + 1)
                S.activation(PT[:, 0:4].rearrange("p h c n -> p (h c n)"), bank(0, 2), ACT.Copy).then_inc(s["ptc"], 1)
                if merge:
                    act_mix(act, blk - 1)
                act_deviation(act, blk)
                if merge:
                    act_norm2(act, blk - 1)

            def dve_block(v, blk, half, merge):
                step = Steps(v, s_vstep, 1 + DVE_C + (blk - 1) * DVE_B)
                if merge:
                    dve_gate(v, blk - 1)
                wait_mixers(v, blk, half)
                for h in range(HB):
                    q = V.tensor_scalar(kdec[:, h, :], z(KB + h * DK, DK, half), outd[:, h:h + 1], None, ALU.mult)
                q.then_inc(s["kdec"], 1)
                step.did(V.tensor_copy(va[:, 1], z(VA, P, half)))
                v.wait_ge(s["t1"], blk + 1)
                V.tensor_tensor(qdT[:].rearrange("p h n -> p (h n)"), bank(1), into[:].rearrange("p h n -> p (h n)"), ALU.mult)
                V.tensor_copy(qbT[:].rearrange("p h n -> p (h n)"), bank(1))
                V.tensor_copy(kaT[:, 1], ps[:, 3, 0:P]).then_inc(s["qkv"], 1)
                v.wait_ge(s["scores"], blk + 1)
                sc = ps[:, 0:4, :].rearrange("p b (h n) -> p (b h) n", h=2)
                V.scalar_tensor_tensor(Pr[:, :, P:], sc[:, :, P:], HD ** -0.5, alibi[:, :, P:], ALU.mult, ALU.add)
                V.scalar_tensor_tensor(Pr[:, :, 0:P], sc[:, :, 0:P], HD ** -0.5, alibi_c[:], ALU.mult, ALU.add).then_inc(s["sm_s"], 1)
                v.wait_ge(s["st"], blk + 1)
                V.tensor_tensor(atm[:].rearrange("p h n -> p (h n)"), bank(6), intra[:].rearrange("p h n -> p (h n)"), ALU.mult).then_inc(s["atm"], 1)
                dve_softmax(v, blk, 2 * P, sink[:], step)
                dve_probs(v, blk, 2 * P)
                if merge:
                    dve_merge(v, blk - 1)
                v.wait_ge(s["pt"], blk + 1)
                V.tensor_copy(PT[:, 4:8].rearrange("p h c n -> p (h c n)"), bank(2, 2)).then_inc(s["ptc"], 1)
                v.wait_ge(s["oat"], blk + 1)
                V.tensor_copy(oaT[:].rearrange("p j n -> p (j n)"), bank(0)).then_inc(s["oatc"], 1)
                V.tensor_copy(kaT[:, 0], kaT[:, 1])
                V.tensor_copy(va[:, 0], va[:, 1])
                V.tensor_copy(alibi_c[:], alibi[:, :, 0:P]).then_inc(s["keep"], 1)
                dve_retention_norm(v, blk, 2, step)
                if merge:
                    dve_residual(v, blk - 1)
                v.wait_ge(s["kvp"], blk)
                for h in range(HB):
                    q = V.scalar_tensor_tensor(st[:, h, :], st[:, h, :], math.exp(P * LOG_DECAY[h]),
                                               ps[:, 4 + h // 2, (h % 2) * DV:(h % 2 + 1) * DV], ALU.mult, ALU.add)
                q.then_inc(s["stn"], 1)
                if merge:
                    dve_norm2(v, blk - 1)
                assert step.n == DVE_B, step.n

            with nc.Block() as block:
                @block.sync
                def _(sp):
                    load_mixers(sp, 1, 1)
                    sp.dma_start(outd[:], t["out_dec"]).then_inc(s_tab, 16)
                    sp.dma_start(into[:].rearrange("p h n -> p (h n)"), t["into"]).then_inc(s_tab, 16)
                    sp.dma_start(alibi[:].rearrange("p h n -> p (h n)"), t["alibi"]).then_inc(s_tab, 16)
                    sp.dma_start(intra[:].rearrange("p h n -> p (h n)"), t["intra"]).then_inc(s_tab, 16)
                    sp.dma_start(sink[:], t["sinks"].to_broadcast([P, HA])).then_inc(s_tab, 16)
                    sp.dma_start(bg[:], t["b_gate"].to_broadcast([P, 2 * D])).then_inc(s_tab, 16)
                    sp.dma_start(gf[:], t["norm_ffn"].to_broadcast([P, D])).then_inc(s_tab, 16)
                    load_gates(sp, 1)
                    sp.dma_start(wa[:], t["w_branch_a"].rearrange("(k p) n -> p k n", p=P)).then_inc(s_wb, 16)
                    sp.dma_start(wb[:], t["w_branch_b"].rearrange("(k p) n -> p k n", p=P)).then_inc(s_wb, 16)
                    sp.dma_start(wo[:], t["w_out"].rearrange("(k p) n -> p k n", p=P)).then_inc(s_wb, 16)
                    for src, dst in ((KA, o["kp"]), (VA, o["vp"])):
                        sp.dma_start(dst, z_d[(NB - 1) * P:, src:src + P]).then_inc(s_copy, 16)
                    load_mixers(sp, 2, 0)
                    with sp.Fori(1, NB // 2) as pair:
                        for half in range(2):
                            blk = 2 * pair + half
                            sp.wait_ge(s["mixt"], blk)
                            load_gates(sp, blk)
                            sp.wait_ge(s["keep"], blk)
                            sp.wait_ge(s["stn"], blk)
                            load_mixers(sp, blk + 1, 1 - half)
                    sp.wait_ge(s["mixt"], NB - 1)
                    load_gates(sp, NB - 1)
                    sp.wait_ge(s["stn"], NB)
                    sp.dma_start(o["sp"].rearrange("(h p) v -> p h v", p=DK), st[:]).then_inc(s_sto, 16)
                    sp.wait_ge(s_sto, 16 * HB + 16)
                    sp.wait_ge(s_copy, 16 * 6)

                @block.gpsimd
                def _(g):
                    load_rows(g, 1)
                    with g.Fori(2, NB) as blk:
                        store_block(g, blk - 1)
                        g.wait_ge(s["x1st"], 16 * blk)
                        g.sem_inc(s_pool, 1)
                        g.wait_ge(s["h2st"], 16 * blk)
                        g.sem_inc(s_pool, 1)
                        load_rows(g, blk)
                    store_block(g, NB - 1)
                    g.wait_ge(s["x1st"], 16 * NB)
                    g.wait_ge(s["h2st"], 16 * NB)

                @block.tensor
                def _(pe):
                    pe_block(pe, 1, 1, False)
                    pe.wait_ge(s_wb, 16 * 5)
                    with pe.Fori(1, NB // 2) as pair:
                        for half in range(2):
                            pe_block(pe, 2 * pair + half, half, True)
                    pe_block(pe, NB - 1, 0, True)
                    pe_gated_transposes(pe, NB - 1)
                    pe_branches(pe, NB - 1)
                    pe_mix_transposes(pe, NB - 1)
                    pe_output(pe, NB - 1)

                @block.scalar
                def _(act):
                    act_block(act, 1, 1, False)
                    with act.Fori(1, NB // 2) as pair:
                        for half in range(2):
                            act_block(act, 2 * pair + half, half, True)
                    act_block(act, NB - 1, 0, True)
                    act_gate(act, NB - 1)
                    act_gated(act, NB - 1)
                    act_sigmoids(act, NB - 1)
                    act_mix(act, NB - 1)
                    act_norm2(act, NB - 1)

                @block.vector
                def _(v):
                    V.memset(kaT[:, 0], 0.0)
                    V.memset(va[:, 0], 0.0)
                    V.memset(alibi_c[:], NEG).then_inc(s["keep"], 1)
                    V.memset(st[:], 0.0).then_inc(s["stn"], 1)
                    v.wait_ge(s_tab, 16 * 7)
                    dve_block(v, 1, 1, False)
                    with v.Fori(1, NB // 2) as pair:
                        for half in range(2):
                            dve_block(v, 2 * pair + half, half, True)
                    dve_block(v, NB - 1, 0, True)
                    dve_gate(v, NB - 1)
                    dve_merge(v, NB - 1)
                    dve_residual(v, NB - 1)
                    dve_norm2(v, NB - 1)

        with ExitStack() as m:
            kt, io, H, hT, SC, VV, II, IF, CA, BV, BP, AU, AF, I12, IX, GT, GS, IXD, GD, DOT, GE, WG, nf, m4 = search_buffers(m, "_p")
            wq = sb(m, "wq", [P, KT, PH * 256])
            Q = sb(m, "Q", [P, 16, P])
            qT = sb(m, "qT", [P, 16, P])
            ring = sb(m, "ring", [P, RING, D])
            ACC = sb(m, "ACC", [P, 2, D])
            X1 = sb(m, "X1", [P, D])
            H2 = sb(m, "H2", [P, D])

            with nc.Block() as block:
                @block.sync
                def _(sp):
                    sp.dma_start(H[:], rows(h2_d, 1)).then_inc(c["hld"], 16)
                    load_search(sp)
                    sp.dma_start(nf[:], t["norm_final"].to_broadcast([P, D])).then_inc(d["nf"], 16)
                    sp.dma_start(X1[:], rows(x1_d, 1)).then_inc(d["x1"], 16)
                    with sp.Fori(2, NB) as blk:
                        sp.wait_ge(c["ht"], blk)
                        sp.wait_ge(c["hcp"], blk)
                        sp.dma_start(H[:], rows(h2_d, blk)).then_inc(c["hld"], 16)
                        sp.wait_ge(d["yo"], blk)
                        sp.dma_start(rows(o["y"], blk - 1), X1[:]).then_inc(d["yst"], 16)
                        sp.wait_ge(d["yst"], 16 * blk)
                        sp.dma_start(X1[:], rows(x1_d, blk)).then_inc(d["x1"], 16)
                    sp.wait_ge(d["yo"], NB)
                    sp.dma_start(rows(o["y"], NB - 1), X1[:]).then_inc(d["yst"], 16)
                    sp.wait_ge(d["yst"], 16 * NB)

                @block.tensor
                def _(pe):
                    pe.wait_ge(s_cw, 32 * (KT + 3))
                    with pe.Fori(1, NB) as blk:
                        pe_keys(pe, blk)

                @block.scalar
                def _(act):
                    act_keys_first(act, 1)
                    act_keys_second(act, 1)
                    act_gates(act, 1)
                    with act.Fori(1, NB - 1) as blk:
                        act_keys_first(act, blk + 1)
                        act_gelu(act, blk, 0)
                        act_keys_second(act, blk + 1)
                        for grp in range(1, 5):
                            act_gelu(act, blk, grp)
                        act_gates(act, blk + 1)
                        for grp in range(5, PH):
                            act_gelu(act, blk, grp)
                        act_norm(act, blk)
                    for grp in range(PH):
                        act_gelu(act, NB - 1, grp)
                    act_norm(act, NB - 1)

                @block.vector
                def _(v):
                    v.wait_ge(s_cw, 32 * (KT + 3))
                    v.wait_ge(d["nf"], 32)
                    step = Steps(v, s_vstep, STEPS_C + DVE_C)
                    for part in range(PARTS):
                        dve_keys(part, v, 1, step)
                    assert step.n == DVE_C, step.n
                    dve_hand_over(v, 1)
                    dve_hand_over_places(v, 1)
                    dve_hand_over_last_places(v)
                    with v.Fori(1, NB - 1) as blk:
                        dve_experts(v, blk, True)
                    dve_experts(v, NB - 1, False)

                @block.gpsimd
                def _(g):
                    with g.Fori(1, NB) as blk:
                        pool_gathers(g, blk)




def kernel(**inputs):
    import concourse.bacc as bacc
    from concourse.bass_utils import run_bass_kernel_spmd

    i = {n: np.asarray(a) for n, a in inputs.items()}
    x = np.concatenate([i["x_sample"].reshape(P, D), i["x_prompt"].reshape(SEQ, D)], 0)
    pair = [h for j in range(GRP) for h in (j, GRP + j)]
    w_in = i["w_in"][0]
    w_in = np.concatenate([w_in[:, :HA * HD].reshape(D, HA, HD)[:, pair].reshape(D, HA * HD), w_in[:, HA * HD:]], 1)
    sinks = i["attn_sinks"][0]
    a = {
        "x": x, "x_t": x.T,
        "w_in": w_in.reshape(KT, P, WT, WC).transpose(2, 1, 0, 3).reshape(WT * P, KT * WC),
        "norm_mix": i["norm_mix"][0].reshape(KT, P).T,
        "b_gate": i["b_gate"], "norm_ffn": i["norm_ffn"], "norm_final": i["norm_final"].reshape(1, D),
        "sinks": sinks.reshape(1, HA), "sinks_rows": np.repeat(sinks, DEC_S).reshape(P, 1),
        "cache_kt": i["cache_swa_k"].reshape(DEC_B * WINDOW, P).T,
        "cache_k": i["cache_swa_k"].reshape(DEC_B * WINDOW, P), "cache_v": i["cache_swa_v"].reshape(DEC_B * WINDOW, P),
        "state": i["state_ret"].reshape(DEC_B * HB * DK, DV),
        "w_branch_a": i["w_branch_a"][0].reshape(HA, HD, D)[pair].reshape(HA * HD, D),
        "w_branch_b": i["w_branch_b"][0], "w_out": i["w_out"][0],
        "peer_w_q": i["peer_w_q"][0], "sub_k1t": i["peer_sub_k1"][0].T, "sub_k2t": i["peer_sub_k2"][0].T,
        "peer_u": i["peer_u"][0], "peer_v": i["peer_v"][0],
    } | shape_tables()
    outs = {"y": (NB * P, D), "kp": (WINDOW, P), "vp": (WINDOW, P), "sp": (HB * DK, DV),
            "kc": (DEC_B * WINDOW, P), "vc": (DEC_B * WINDOW, P), "ss": (DEC_B * HB * DK, DV)}
    nc = bacc.Bacc("TRN2", target_bir_lowering=False, num_devices=1)
    arrays, t, o = {}, {}, {}
    for n, v in a.items():
        arrays[f"in_{n}"] = np.ascontiguousarray(v)
        t[n] = nc.dram_tensor(f"in_{n}", v.shape, mybir.dt.from_np(v.dtype), kind="ExternalInput").ap()
    for n, shape in outs.items():
        o[n] = nc.dram_tensor(f"out_{n}", shape, f32, kind="ExternalOutput").ap()
    trunk_kernel(nc, t, o)
    r = run_bass_kernel_spmd(nc, [arrays], core_ids=[0]).results[0]
    g = {n: r[f"out_{n}"] for n in outs}
    return (g["y"][P:].reshape(1, SEQ, D), g["y"][:P].reshape(DEC_B, DEC_S, D),
            g["kp"].reshape(1, 1, WINDOW, KV, HD), g["vp"].reshape(1, 1, WINDOW, KV, HD), g["sp"].reshape(1, 1, HB, DK, DV),
            g["kc"].reshape(1, DEC_B, WINDOW, KV, HD), g["vc"].reshape(1, DEC_B, WINDOW, KV, HD), g["ss"].reshape(1, DEC_B, HB, DK, DV))
```
